# Optimizing a Trainium2 kernel written in Bass

```python
import math
import jax, jax.numpy as jnp
from jax import lax
import numpy as np

D_MODEL = 1024
BATCH = 1
SEQ = 256
DEPTH = 2

MEM_LEN = 256
RMS_EPS = 1e-6
ROPE_THETA = 500000.0
ROPE_FRACTION = 4
Q_BLOCK = 128
MOBA_HEADS = 6
MOBA_DIM = 64
MOBA_BLOCK = 256
MOBA_TOPK = 3
MOBA_Q_BLOCK = 64
DIFF_HEADS = 4
DIFF_QK_DIM = 32
DIFF_V_DIM = 64
SB_HEADS = 6
SB_DIM = 64
XATTN_HEADS = 4
XATTN_DIM = 128

MOBA_W = MOBA_HEADS * MOBA_DIM
DIFF_QK_W = DIFF_HEADS * 2 * DIFF_QK_DIM
DIFF_W = DIFF_HEADS * DIFF_V_DIM
SB_W = SB_HEADS * SB_DIM
D_MIX = MOBA_W + DIFF_W + SB_W
IN_SPLIT_SIZES = (MOBA_W, MOBA_W, MOBA_W, MOBA_W,
                  DIFF_QK_W, DIFF_QK_W, DIFF_W, DIFF_W,
                  SB_W, SB_W, SB_W, SB_W)
D_IN = 4 * MOBA_W + 2 * DIFF_QK_W + 2 * DIFF_W + 4 * SB_W
XATTN_W = XATTN_HEADS * XATTN_DIM


def rms_norm(x, g):
    xf = x.astype(jnp.float32)
    y = xf * lax.rsqrt(jnp.mean(xf * xf, axis=-1, keepdims=True) + RMS_EPS)
    return (y * g.astype(jnp.float32)).astype(x.dtype)

def to_heads(t, n_heads, d):
    b, s, _ = t.shape
    return t.reshape(b, s, n_heads, d).transpose(0, 2, 1, 3)

def from_heads(t):
    b, h, s, d = t.shape
    return t.transpose(0, 2, 1, 3).reshape(b, s, h * d)

def rope_tables(positions, head_dim):
    rot = head_dim // ROPE_FRACTION
    inv = 1.0 / (ROPE_THETA ** (jnp.arange(0, rot, 2, dtype=jnp.float32) / rot))
    ang = positions.astype(jnp.float32)[..., None] * inv
    return jnp.cos(ang)[:, None], jnp.sin(ang)[:, None]

def apply_partial_rope(x, cos, sin):
    r2 = cos.shape[-1]
    c = cos.astype(x.dtype)
    s = sin.astype(x.dtype)
    x1 = x[..., :r2]
    x2 = x[..., r2:2 * r2]
    return jnp.concatenate([x1 * c - x2 * s, x2 * c + x1 * s, x[..., 2 * r2:]], axis=-1)

def sweep_blocks(fn, seq, qb):
    out = lax.map(fn, jnp.arange(seq // qb))
    n, b, h, _, d = out.shape
    return out.transpose(1, 2, 0, 3, 4).reshape(b, h, n * qb, d)

def moba_attention(q, k, v):
    b, h, s, d = q.shape
    nb = -(-s // MOBA_BLOCK)
    pad = nb * MOBA_BLOCK - s
    kp = jnp.pad(k, ((0, 0), (0, 0), (0, pad), (0, 0)))
    vp = jnp.pad(v, ((0, 0), (0, 0), (0, pad), (0, 0)))
    kb = kp.reshape(b, h, nb, MOBA_BLOCK, d)
    vb = vp.reshape(b, h, nb, MOBA_BLOCK, d)
    k_mean = jnp.mean(kb.astype(jnp.float32), axis=3)
    n_sel = min(MOBA_TOPK, nb)
    scale = d ** -0.5
    bi = jnp.arange(b)[:, None, None, None]
    hi = jnp.arange(h)[None, :, None, None]

    def block(i):
        q0 = i * MOBA_Q_BLOCK
        qi = lax.dynamic_slice_in_dim(q, q0, MOBA_Q_BLOCK, axis=2)
        own = q0 // MOBA_BLOCK
        tq = q0 + jnp.arange(MOBA_Q_BLOCK)
        gate = jnp.einsum('bhqd,bhnd->bhqn', qi.astype(jnp.float32), k_mean)
        gate = jnp.where(jnp.arange(nb) < own, gate, -jnp.inf)
        _, idx = lax.top_k(gate, n_sel)
        valid = idx < own
        ks = kb[bi, hi, idx]
        vs = vb[bi, hi, idx]
        s_sel = jnp.einsum('bhqd,bhqnld->bhqnl', qi, ks).astype(jnp.float32) * scale
        s_sel = jnp.where(valid[..., None], s_sel, -jnp.inf)
        s_sel = s_sel.reshape(b, h, MOBA_Q_BLOCK, n_sel * MOBA_BLOCK)
        ko = lax.dynamic_slice_in_dim(kp, own * MOBA_BLOCK, MOBA_BLOCK, axis=2)
        vo = lax.dynamic_slice_in_dim(vp, own * MOBA_BLOCK, MOBA_BLOCK, axis=2)
        s_own = jnp.einsum('bhqd,bhld->bhql', qi, ko).astype(jnp.float32) * scale
        to = own * MOBA_BLOCK + jnp.arange(MOBA_BLOCK)
        s_own = jnp.where(to[None, :] <= tq[:, None], s_own, -jnp.inf)
        p = jax.nn.softmax(jnp.concatenate([s_sel, s_own], axis=-1), axis=-1)
        p_sel = p[..., :n_sel * MOBA_BLOCK].reshape(b, h, MOBA_Q_BLOCK, n_sel, MOBA_BLOCK).astype(v.dtype)
        p_own = p[..., n_sel * MOBA_BLOCK:].astype(v.dtype)
        return (jnp.einsum('bhqnl,bhqnld->bhqd', p_sel, vs)
                + jnp.einsum('bhql,bhld->bhqd', p_own, vo))

    return sweep_blocks(block, s, MOBA_Q_BLOCK)

def diff_attention(q, k, v, lam, head_norm_g, lam_init):
    b, h2, s, dq = q.shape
    h = h2 // 2
    scale = dq ** -0.5
    kpos = jnp.arange(s)

    def block(i):
        q0 = i * Q_BLOCK
        qi = lax.dynamic_slice_in_dim(q, q0, Q_BLOCK, axis=2)
        sc = jnp.einsum('bhqd,bhkd->bhqk', qi, k).astype(jnp.float32) * scale
        mask = kpos[None, :] <= (q0 + jnp.arange(Q_BLOCK))[:, None]
        p = jax.nn.softmax(jnp.where(mask, sc, -jnp.inf), axis=-1).reshape(b, h, 2, Q_BLOCK, s)
        a = p[:, :, 0] - lam * p[:, :, 1]
        return jnp.einsum('bhqk,bhkd->bhqd', a.astype(v.dtype), v)

    o = sweep_blocks(block, s, Q_BLOCK)
    o = rms_norm(o, head_norm_g)
    return o * (1.0 - lam_init)

def stick_breaking_attention(q, k, v):
    b, h, s, d = q.shape
    scale = d ** -0.5
    kpos = jnp.arange(s)

    def block(i):
        q0 = i * Q_BLOCK
        qi = lax.dynamic_slice_in_dim(q, q0, Q_BLOCK, axis=2)
        z = jnp.einsum('bhqd,bhkd->bhqk', qi, k).astype(jnp.float32) * scale
        mask = kpos[None, :] < (q0 + jnp.arange(Q_BLOCK))[:, None]
        log_beta = jax.nn.log_sigmoid(z)
        log_1m_beta = jnp.where(mask, log_beta - z, 0.0)
        between = lax.cumsum(log_1m_beta, axis=3, reverse=True) - log_1m_beta
        w = jnp.where(mask, jnp.exp(log_beta + between), 0.0)
        return jnp.einsum('bhqk,bhkd->bhqd', w.astype(v.dtype), v)

    return sweep_blocks(block, s, Q_BLOCK)

def hybrid_mixer(hn, rope64, rope32, w_in, w_out, lq1, lk1, lq2, lk2, head_norm_g, lam_init):
    proj = hn @ w_in
    cuts = list(np.cumsum(IN_SPLIT_SIZES)[:-1])
    (mq, mk, mv, mg, dq_, dk_, dv_, dg, sq, sk, sv, sg) = jnp.split(proj, cuts, axis=-1)
    cos64, sin64 = rope64
    a_q = apply_partial_rope(to_heads(mq, MOBA_HEADS, MOBA_DIM), cos64, sin64)
    a_k = apply_partial_rope(to_heads(mk, MOBA_HEADS, MOBA_DIM), cos64, sin64)
    a_o = moba_attention(a_q, a_k, to_heads(mv, MOBA_HEADS, MOBA_DIM))
    cos32, sin32 = rope32
    b_q = apply_partial_rope(to_heads(dq_, 2 * DIFF_HEADS, DIFF_QK_DIM), cos32, sin32)
    b_k = apply_partial_rope(to_heads(dk_, 2 * DIFF_HEADS, DIFF_QK_DIM), cos32, sin32)
    f32 = jnp.float32
    lam = (jnp.exp(jnp.sum(lq1.astype(f32) * lk1.astype(f32)))
           - jnp.exp(jnp.sum(lq2.astype(f32) * lk2.astype(f32))) + lam_init)
    b_o = diff_attention(b_q, b_k, to_heads(dv_, DIFF_HEADS, DIFF_V_DIM), lam, head_norm_g, lam_init)
    c_o = stick_breaking_attention(to_heads(sq, SB_HEADS, SB_DIM), to_heads(sk, SB_HEADS, SB_DIM),
                                   to_heads(sv, SB_HEADS, SB_DIM))
    merged = jnp.concatenate([from_heads(a_o) * jax.nn.silu(mg),
                              from_heads(b_o).astype(hn.dtype) * jax.nn.silu(dg),
                              from_heads(c_o) * jax.nn.silu(sg)], axis=-1)
    return merged @ w_out

def memory_cross_attention(hn, mem_n, w_xq, w_xkv, w_xo):
    q = to_heads(hn @ w_xq, XATTN_HEADS, XATTN_DIM)
    k, v = jnp.split(mem_n @ w_xkv, 2, axis=-1)
    k = to_heads(k, XATTN_HEADS, XATTN_DIM)
    v = to_heads(v, XATTN_HEADS, XATTN_DIM)
    sc = jnp.einsum('bhsd,bhmd->bhsm', q, k).astype(jnp.float32) * (XATTN_DIM ** -0.5)
    p = jax.nn.softmax(sc, axis=-1).astype(v.dtype)
    o = jnp.einsum('bhsm,bhmd->bhsd', p, v)
    return from_heads(o) @ w_xo

def first_inputs(seed: int = 0) -> dict:
    key = jax.random.key(seed)
    ks = jax.random.split(key, 20)
    f32 = jnp.float32

    def w(k, shape, fan_in):
        return jax.random.normal(k, shape, f32) * (fan_in ** -0.5)

    def gain(k, shape):
        return 1.0 + 0.02 * jax.random.normal(k, shape, f32)

    offsets = jax.random.randint(ks[2], (BATCH, 1), 0, 4096, dtype=jnp.int32)
    positions = offsets + jnp.arange(SEQ, dtype=jnp.int32)[None, :]
    return {
        "x": jax.random.normal(ks[0], (BATCH, SEQ, D_MODEL), f32),
        "mem": jax.random.normal(ks[1], (BATCH, MEM_LEN, D_MODEL), f32),
        "positions": positions,
        "attn_norm_g": gain(ks[3], (DEPTH, D_MODEL)),
        "w_in": w(ks[4], (DEPTH, D_MODEL, D_IN), D_MODEL),
        "w_out": w(ks[5], (DEPTH, D_MIX, D_MODEL), D_MIX),
        "diff_lambda_q1": 0.1 * jax.random.normal(ks[6], (DEPTH, DIFF_QK_DIM), f32),
        "diff_lambda_k1": 0.1 * jax.random.normal(ks[7], (DEPTH, DIFF_QK_DIM), f32),
        "diff_lambda_q2": 0.1 * jax.random.normal(ks[8], (DEPTH, DIFF_QK_DIM), f32),
        "diff_lambda_k2": 0.1 * jax.random.normal(ks[9], (DEPTH, DIFF_QK_DIM), f32),
        "diff_head_norm_g": gain(ks[10], (DEPTH, DIFF_V_DIM)),
        "xattn_norm_g": gain(ks[11], (DEPTH, D_MODEL)),
        "mem_norm_g": gain(ks[12], (DEPTH, D_MODEL)),
        "w_xq": w(ks[13], (DEPTH, D_MODEL, XATTN_W), D_MODEL),
        "w_xkv": w(ks[14], (DEPTH, D_MODEL, 2 * XATTN_W), D_MODEL),
        "w_xo": w(ks[15], (DEPTH, XATTN_W, D_MODEL), XATTN_W),
        "final_norm_g": gain(ks[16], (D_MODEL,)),
    }

def first_block(x, mem, positions, attn_norm_g, w_in, w_out, diff_lambda_q1, diff_lambda_k1,
              diff_lambda_q2, diff_lambda_k2, diff_head_norm_g, xattn_norm_g, mem_norm_g,
              w_xq, w_xkv, w_xo, final_norm_g):
    rope64 = rope_tables(positions, MOBA_DIM)
    rope32 = rope_tables(positions, DIFF_QK_DIM)
    h = x
    for l in range(DEPTH):
        lam_init = 0.8 - 0.6 * math.exp(-0.3 * l)
        hn = rms_norm(h, attn_norm_g[l])
        h = h + hybrid_mixer(hn, rope64, rope32, w_in[l], w_out[l],
                             diff_lambda_q1[l], diff_lambda_k1[l], diff_lambda_q2[l], diff_lambda_k2[l],
                             diff_head_norm_g[l], lam_init)
        h = h + memory_cross_attention(rms_norm(h, xattn_norm_g[l]), rms_norm(mem, mem_norm_g[l]),
                                       w_xq[l], w_xkv[l], w_xo[l])
    return rms_norm(h, final_norm_g)


CHUNK = 64
N_META = 16
META_PAD = CHUNK - N_META
HEAD_DIM = 64
A_HEADS = 8
IDX_HEADS = 8
IDX_DIM = 64
DSA_MAX_K = 256
A_QBLK = 64
B_HEADS = 8
B_VDIM = 2 * HEAD_DIM
C_HEADS = 8
C_KV_HEADS = 2
C_WINDOW = 128
C_WIN_CHUNKS = C_WINDOW // CHUNK
D_WIDTH = 512
POOL_WINDOWS = (2, 4, 8, 16)
D_GROUP = D_WIDTH // len(POOL_WINDOWS)
D_FF = 2816
EPS = 1e-6
NEG = -1e30

EVEN_SIZES = ([A_HEADS * HEAD_DIM] * 3 + [IDX_HEADS * IDX_DIM, IDX_DIM, IDX_HEADS]
              + [B_HEADS * HEAD_DIM] * 2 + [B_HEADS * B_VDIM] * 2)
EVEN_IN = sum(EVEN_SIZES)
EVEN_OUT = A_HEADS * HEAD_DIM + B_HEADS * B_VDIM
ODD_SIZES = [C_HEADS * HEAD_DIM, C_KV_HEADS * HEAD_DIM, C_KV_HEADS * HEAD_DIM, D_WIDTH]
ODD_IN = sum(ODD_SIZES)
ODD_OUT = C_HEADS * HEAD_DIM + D_WIDTH
N_EVEN = (DEPTH + 1) // 2
N_ODD = DEPTH // 2


def rms_norm_2(x, gain=None):
    xf = x.astype(jnp.float32)
    y = xf * lax.rsqrt(jnp.mean(xf * xf, axis=-1, keepdims=True) + EPS)
    if gain is not None:
        y = y * gain.astype(jnp.float32)
    return y.astype(x.dtype)

def swiglu(x, w_in, w_out):
    g, u = jnp.split(x @ w_in, 2, axis=-1)
    return (jax.nn.silu(g) * u) @ w_out

def split_cols(a, sizes):
    out, off = [], 0
    for s in sizes:
        out.append(a[..., off:off + s])
        off += s
    return out

def chunk_ids(n):
    return (jnp.arange(n) + META_PAD) // CHUNK

def pad_left(a):
    return jnp.pad(a, [(0, 0), (META_PAD, 0)] + [(0, 0)] * (a.ndim - 2))

def dsa_attention(q, k, v, iq, ik, iw, top_k):
    B, L, H, dh = q.shape
    cid = chunk_ids(L)
    nb = -(-L // A_QBLK)
    padn = nb * A_QBLK - L

    def blocks(a):
        a = jnp.pad(a, [(0, 0), (0, padn)] + [(0, 0)] * (a.ndim - 2))
        return jnp.moveaxis(a.reshape((B, nb, A_QBLK) + a.shape[2:]), 1, 0)

    q_cid = chunk_ids(nb * A_QBLK).reshape(nb, A_QBLK)
    iw = iw * (IDX_HEADS ** -0.5 * IDX_DIM ** -0.5)
    gather = jax.vmap(lambda t, i: t[i])

    def one_block(args):
        qb, iqb, iwb, qc = args
        logits = jnp.einsum('bqhd,bsd->bqhs', iqb, ik)
        score = jnp.einsum('bqh,bqhs->bqs', iwb, jax.nn.relu(logits)).astype(jnp.float32)
        adm = cid[None, :] <= qc[:, None]
        score = jnp.where(adm[None], score, NEG)
        _, idx = lax.top_k(score, top_k)
        valid = cid[idx] <= qc[None, :, None]
        kg = gather(k, idx)
        vg = gather(v, idx)
        s = jnp.einsum('bqhd,bqkhd->bhqk', qb, kg).astype(jnp.float32) * dh ** -0.5
        s = jnp.where(valid[:, None], s, NEG)
        p = jax.nn.softmax(s, axis=-1).astype(v.dtype)
        return jnp.einsum('bhqk,bqkhd->bqhd', p, vg)

    out = lax.map(one_block, (blocks(q), blocks(iq), blocks(iw), q_cid))
    return jnp.moveaxis(out, 0, 1).reshape(B, nb * A_QBLK, H, dh)[:, :L]

def rotary(x, pos):
    d = x.shape[-1]
    inv = 1.0 / (10000.0 ** (jnp.arange(0, d, 2, dtype=jnp.float32) / d))
    ang = pos.astype(jnp.float32)[:, None] * inv[None]
    cos = jnp.cos(ang)[None, :, None, :]
    sin = jnp.sin(ang)[None, :, None, :]
    x1, x2 = jnp.split(x.astype(jnp.float32), 2, axis=-1)
    return jnp.concatenate([x1 * cos - x2 * sin, x1 * sin + x2 * cos], axis=-1).astype(x.dtype)

def retention(q, k, v):
    B, Lp, H, dk = q.shape
    dv = v.shape[-1]
    N = Lp // CHUNK
    pos = jnp.arange(Lp) - META_PAD
    q = rotary(q, pos)
    k = rotary(k, pos) * dk ** -0.5
    log_g = jnp.log(1.0 - 2.0 ** (-5.0 - jnp.arange(H, dtype=jnp.float32)))
    i = jnp.arange(CHUNK, dtype=jnp.float32)
    rel = i[:, None] - i[None, :]
    dmat = jnp.where(rel >= 0, jnp.exp(jnp.maximum(rel, 0.0)[None] * log_g[:, None, None]), 0.0)
    q_dec = jnp.exp((i + 1.0)[:, None] * log_g[None])
    k_dec = jnp.exp((CHUNK - 1.0 - i)[:, None] * log_g[None])
    c_dec = jnp.exp(CHUNK * log_g)
    qc = q.reshape(B, N, CHUNK, H, dk)
    kc = k.reshape(B, N, CHUNK, H, dk)
    vc = v.reshape(B, N, CHUNK, H, dv)
    inner = jnp.einsum('bnihd,bnjhd->bnhij', qc, kc) * dmat.astype(q.dtype)
    inner = jnp.einsum('bnhij,bnjhe->bnihe', inner, vc)

    def step(S, xs):
        qn, kn, vn = xs
        cross = jnp.einsum('bihd,bhde->bihe', qn, S) * q_dec[None, :, :, None]
        S = S * c_dec[None, :, None, None] + jnp.einsum(
            'bjhd,bjhe->bhde', kn * k_dec[None, :, :, None], vn)
        return S, cross

    S0 = jnp.zeros((B, H, dk, dv), jnp.float32)
    _, cross = lax.scan(step, S0, (jnp.moveaxis(qc, 1, 0), jnp.moveaxis(kc, 1, 0),
                                   jnp.moveaxis(vc, 1, 0)))
    out = inner + jnp.moveaxis(cross, 0, 1).astype(inner.dtype)
    return out.reshape(B, Lp, H, dv)

def swa_sinks(q, k, v, sinks):
    B, Lp, H, dh = q.shape
    G = k.shape[2]
    R = H // G
    N = Lp // CHUNK
    W = C_WIN_CHUNKS

    def band(t):
        tc = t.reshape(B, N, CHUNK, G, dh)
        tp = jnp.pad(tc, ((0, 0), (W, 0), (0, 0), (0, 0), (0, 0)))
        bnd = jnp.concatenate([tp[:, j:j + N] for j in range(W + 1)], axis=2)
        meta = jnp.broadcast_to(t[:, META_PAD:CHUNK][:, None], (B, N, N_META, G, dh))
        return jnp.concatenate([meta, bnd], axis=2)

    kb, vb = band(k), band(v)
    key_chunk = jnp.arange(N)[:, None] - W + (jnp.arange((W + 1) * CHUNK) // CHUNK)[None]
    valid = jnp.concatenate([jnp.ones((N, N_META), bool), key_chunk >= 1], axis=1)
    qg = q.reshape(B, N, CHUNK, G, R, dh)
    s = jnp.einsum('bncgrd,bnkgd->bngrck', qg, kb).astype(jnp.float32) * dh ** -0.5
    s = jnp.where(valid[None, :, None, None, None, :], s, NEG)
    sink = jnp.broadcast_to(sinks.reshape(G, R).astype(jnp.float32)[None, None, :, :, None, None],
                            s.shape[:-1] + (1,))
    p = jax.nn.softmax(jnp.concatenate([s, sink], axis=-1), axis=-1)[..., :-1].astype(v.dtype)
    out = jnp.einsum('bngrck,bnkgd->bncgrd', p, vb)
    return out.reshape(B, Lp, H, dh)

def pool_mixer(x, d_mix, d_scale):
    B, L, _ = x.shape
    xg = x.astype(jnp.float32).reshape(B, L, len(POOL_WINDOWS), D_GROUP)
    cs = jnp.pad(jnp.cumsum(xg, axis=1), ((0, 0), (1, 0), (0, 0), (0, 0)))
    t = jnp.arange(L)
    pooled = []
    for gi, w in enumerate(POOL_WINDOWS):
        c = cs[:, :, gi]
        lag = jnp.pad(c, ((0, 0), (w, 0), (0, 0)))[:, 1:L + 1]
        cnt = jnp.minimum(t + 1, w).astype(jnp.float32)[None, :, None]
        pooled.append((c[:, 1:] - lag) / cnt)
    pooled = jnp.stack(pooled, axis=2)
    y = (pooled - xg).astype(x.dtype)
    y = jnp.einsum('blgc,gce->blge', y, d_mix).reshape(B, L, D_WIDTH)
    return y * d_scale

def even_mixer(h, w_in, a_qn, a_kn, w_out, top_k):
    B, L, _ = h.shape
    aq, ak, av, iq, ik, iw, bq, bk, bv, bg = split_cols(h @ w_in, EVEN_SIZES)
    hd = lambda t, n: t.reshape(B, L, n, -1)
    aq = rms_norm_2(hd(aq, A_HEADS), a_qn)
    ak = rms_norm_2(hd(ak, A_HEADS), a_kn)
    ya = dsa_attention(aq, ak, hd(av, A_HEADS), hd(iq, IDX_HEADS), ik, iw, top_k)
    ya = ya.reshape(B, L, -1)
    yb = retention(pad_left(hd(bq, B_HEADS)), pad_left(hd(bk, B_HEADS)),
                   pad_left(hd(bv, B_HEADS)))[:, META_PAD:]
    yb = rms_norm_2(yb).astype(h.dtype).reshape(B, L, -1) * jax.nn.silu(bg)
    return jnp.concatenate([ya, yb], axis=-1) @ w_out

def odd_mixer(h, w_in, c_qn, c_kn, c_sinks, d_mix, d_scale, w_out):
    B, L, _ = h.shape
    cq, ck, cv, dx = split_cols(h @ w_in, ODD_SIZES)
    hd = lambda t, n: t.reshape(B, L, n, -1)
    cq = rms_norm_2(hd(cq, C_HEADS), c_qn)
    ck = rms_norm_2(hd(ck, C_KV_HEADS), c_kn)
    yc = swa_sinks(pad_left(cq), pad_left(ck), pad_left(hd(cv, C_KV_HEADS)), c_sinks)
    yc = yc[:, META_PAD:].reshape(B, L, -1)
    yd = pool_mixer(dx, d_mix, d_scale)
    return jnp.concatenate([yc, yd], axis=-1) @ w_out

def second_inputs(seed: int = 0) -> dict:
    key = jax.random.key(seed)
    ks = jax.random.split(key, 21)
    f32 = jnp.float32
    nrm = lambda k, shape, fan: jax.random.normal(k, shape, f32) * fan ** -0.5
    gain = lambda k, shape: 1.0 + 0.05 * jax.random.normal(k, shape, f32)
    return {
        "x": jax.random.normal(ks[0], (BATCH, SEQ, D_MODEL), f32),
        "meta_tokens": jax.random.normal(ks[1], (N_META, D_MODEL), f32),
        "ffn1_norm": gain(ks[2], (DEPTH, D_MODEL)),
        "ffn1_w_in": nrm(ks[3], (DEPTH, D_MODEL, 2 * D_FF), D_MODEL),
        "ffn1_w_out": nrm(ks[4], (DEPTH, D_FF, D_MODEL), D_FF),
        "mix_norm": gain(ks[5], (DEPTH, D_MODEL)),
        "ffn2_norm": gain(ks[6], (DEPTH, D_MODEL)),
        "ffn2_w_in": nrm(ks[7], (DEPTH, D_MODEL, 2 * D_FF), D_MODEL),
        "ffn2_w_out": nrm(ks[8], (DEPTH, D_FF, D_MODEL), D_FF),
        "ev_w_in": nrm(ks[9], (N_EVEN, D_MODEL, EVEN_IN), D_MODEL),
        "ev_a_q_norm": gain(ks[10], (N_EVEN, HEAD_DIM)),
        "ev_a_k_norm": gain(ks[11], (N_EVEN, HEAD_DIM)),
        "ev_w_out": nrm(ks[12], (N_EVEN, EVEN_OUT, D_MODEL), EVEN_OUT),
        "od_w_in": nrm(ks[13], (N_ODD, D_MODEL, ODD_IN), D_MODEL),
        "od_c_q_norm": gain(ks[14], (N_ODD, HEAD_DIM)),
        "od_c_k_norm": gain(ks[15], (N_ODD, HEAD_DIM)),
        "od_c_sinks": 0.5 * jax.random.normal(ks[16], (N_ODD, C_HEADS), f32),
        "od_d_mix": nrm(ks[17], (N_ODD, len(POOL_WINDOWS), D_GROUP, D_GROUP), D_GROUP),
        "od_d_scale": gain(ks[18], (N_ODD, D_WIDTH)),
        "od_w_out": nrm(ks[19], (N_ODD, ODD_OUT, D_MODEL), ODD_OUT),
    }

def second_block(x, meta_tokens, ffn1_norm, ffn1_w_in, ffn1_w_out, mix_norm, ffn2_norm,
              ffn2_w_in, ffn2_w_out, ev_w_in, ev_a_q_norm, ev_a_k_norm, ev_w_out,
              od_w_in, od_c_q_norm, od_c_k_norm, od_c_sinks, od_d_mix, od_d_scale,
              od_w_out):
    B, S, D = x.shape
    top_k = min(DSA_MAX_K, S // 4)
    h = jnp.concatenate([jnp.broadcast_to(meta_tokens.astype(x.dtype)[None], (B, N_META, D)), x],
                        axis=1)
    for layer in range(DEPTH):
        h = h + (0.5 * swiglu(rms_norm_2(h, ffn1_norm[layer]), ffn1_w_in[layer],
                              ffn1_w_out[layer])).astype(h.dtype)
        hn = rms_norm_2(h, mix_norm[layer])
        if layer % 2 == 0:
            e = layer // 2
            y = even_mixer(hn, ev_w_in[e], ev_a_q_norm[e], ev_a_k_norm[e], ev_w_out[e], top_k)
        else:
            o = layer // 2
            y = odd_mixer(hn, od_w_in[o], od_c_q_norm[o], od_c_k_norm[o], od_c_sinks[o],
                          od_d_mix[o], od_d_scale[o], od_w_out[o])
        h = h + y.astype(h.dtype)
        h = h + (0.5 * swiglu(rms_norm_2(h, ffn2_norm[layer]), ffn2_w_in[layer],
                              ffn2_w_out[layer])).astype(h.dtype)
    return h[:, N_META:]


def setup_inputs(seed=0):
    out = dict(first_inputs(seed))
    for name, value in second_inputs(seed + 1).items():
        if name != "x":
            out[name + "_2"] = value
    return out


def reference(
    x, mem, positions, attn_norm_g, w_in, w_out, diff_lambda_q1, diff_lambda_k1, diff_lambda_q2,
    diff_lambda_k2, diff_head_norm_g, xattn_norm_g, mem_norm_g, w_xq, w_xkv, w_xo, final_norm_g,
    meta_tokens_2, ffn1_norm_2, ffn1_w_in_2, ffn1_w_out_2, mix_norm_2, ffn2_norm_2, ffn2_w_in_2,
    ffn2_w_out_2, ev_w_in_2, ev_a_q_norm_2, ev_a_k_norm_2, ev_w_out_2, od_w_in_2, od_c_q_norm_2,
    od_c_k_norm_2, od_c_sinks_2, od_d_mix_2, od_d_scale_2, od_w_out_2,
):
    x = first_block(
        x, mem, positions, attn_norm_g, w_in, w_out, diff_lambda_q1, diff_lambda_k1,
        diff_lambda_q2, diff_lambda_k2, diff_head_norm_g, xattn_norm_g, mem_norm_g, w_xq, w_xkv,
        w_xo, final_norm_g,
    )
    return second_block(
        x, meta_tokens_2, ffn1_norm_2, ffn1_w_in_2, ffn1_w_out_2, mix_norm_2, ffn2_norm_2,
        ffn2_w_in_2, ffn2_w_out_2, ev_w_in_2, ev_a_q_norm_2, ev_a_k_norm_2, ev_w_out_2,
        od_w_in_2, od_c_q_norm_2, od_c_k_norm_2, od_c_sinks_2, od_d_mix_2, od_d_scale_2,
        od_w_out_2,
    )


_drawn_inputs = setup_inputs


def setup_inputs(seed=0):
    import zlib

    import numpy as np

    out = dict(_drawn_inputs(seed))
    spreads = {}
    factors = {'diff_lambda_q1': 5.412,
     'diff_head_norm_g': 3.951,
     'xattn_norm_g': 7.955,
     'mem_norm_g': 5.571,
     'ev_a_q_norm_2': 8.0,
     'ev_a_k_norm_2': 8.0,
     'od_c_q_norm_2': 8.0,
     'od_c_k_norm_2': 8.0,
     'od_c_sinks_2': 8.0,
     'od_d_scale_2': 3.012}
    for name, (base, spread) in spreads.items():
        noise = np.random.default_rng([zlib.crc32(name.encode()), seed]).standard_normal(out[name].shape)
        drawn = base * np.exp(spread * noise) if base else spread * noise
        out[name] = __import__('jax').numpy.asarray(drawn.astype(out[name].dtype))
    for name, factor in factors.items():
        out[name] = (out[name] * factor).astype(out[name].dtype)
    return out
```

```python
import math
from contextlib import ExitStack

import numpy as np

import concourse.bass as bass
from concourse import mybir

F32 = mybir.dt.float32
FR = mybir.dt.float32r
I32 = mybir.dt.int32
ACT = mybir.ActivationFunctionType
ALU = mybir.AluOpType
AX = mybir.AxisListType

P = 128
D = 1024
KC = D // P
SEQ = 256
META = 16
TOK = META + SEQ
DEPTH = 2
CHUNK = 64
META_PAD = CHUNK - META
NEG = -1e30
GONE = -3e38

MOBA_H, DIFF_H, SB_H, X_H = 6, 4, 6, 4
MOBA_T, DIFF_T, SB_T = 3, 2, 3
D_FF = 2816
FT = D_FF // P
A_H, IDX_H, B_H, C_H = 8, 8, 8, 8
TOP_K = min(256, SEQ // 4)
EPS = 1e-6
SLAB = 1024

KB2 = [(0, 128), (128, 128), (256, 16)]


def rope_frequencies(theta, rot):
    return np.float32(1) / np.power(np.float32(theta), np.arange(0, rot, 2, dtype=np.float32) / np.float32(rot))


def signed_swap(head, half):
    m = np.zeros((P, P), np.float32)
    for b in range(0, P, head):
        for i in range(half):
            m[b + half + i, b + i] = -1.0
            m[b + i, b + half + i] = 1.0
    return m


def frequency_column(theta, head, rot):
    inv = rope_frequencies(theta, rot)
    col = np.zeros((P, 1), np.float32)
    for b in range(0, P, head):
        col[b:b + rot // 2, 0] = inv
        col[b + rot // 2:b + rot, 0] = inv
    return col


def constant_tables():
    i = np.arange(P)
    ident = np.eye(P, dtype=np.float32)
    ones = np.ones((P, P), np.float32)
    pair = (i[:, None] // 64 == i[None, :] // 64).astype(np.float32)
    later = (i[:, None] > i[None, :]).astype(np.float32)
    causal = np.concatenate([np.zeros((P, P)), np.where(i[None, :] <= i[:, None], 0.0, NEG)], 1)
    strict = (i[:, None] < i[None, :]).astype(np.float32)
    sb = np.concatenate([strict, ones, strict], 1)
    parts = [("ident", ident), ("ones", ones), ("pair", pair), ("later", later),
             ("swap64", signed_swap(64, 8)), ("swap32", signed_swap(32, 4)), ("swapr", signed_swap(64, 32)),
             ("causal", causal), ("sb", sb),
             ("inv64", frequency_column(500000.0, 64, 16)), ("inv32", frequency_column(500000.0, 32, 8)),
             ("eps", np.full((P, 1), EPS))]
    return parts


def even_tables():
    t = np.arange(TOK)
    cid = (t + META_PAD) // CHUNK
    adm = np.where(cid[None, :] <= cid[:, None], 0.0, NEG)
    adm = np.concatenate([adm, np.zeros((3 * P - TOK, TOK))], 0).reshape(3, P, TOK).transpose(1, 0, 2).reshape(P, 3 * TOK)
    inv = rope_frequencies(10000.0, 64)
    ang = t.astype(np.float32)[None, :] * inv[:, None]
    cos = np.cos(ang).astype(np.float32)[i4]
    sin = np.sin(ang).astype(np.float32)[i4]
    scale = np.float32(0.125)
    return [("adm", adm), ("cosq", cos), ("sinq", sin), ("cosk", cos * scale), ("sink", sin * scale)]


i4 = np.arange(P) % 32


def decay_tables():
    out = np.zeros((P, B_H, 432), np.float64)
    t = np.arange(TOK)
    for h in range(B_H):
        log_g = math.log(1.0 - 2.0 ** (-5.0 - h))
        at = 0
        for s0, n in KB2:
            rel = t[None, s0:] - t[s0:s0 + n, None]
            out[:n, h, at:at + TOK - s0] = np.where(rel >= 0, np.exp(np.maximum(rel, 0) * log_g), 0.0)
            at += TOK - s0
    return out.reshape(P, B_H * 432)


def window_tables():
    t = np.arange(TOK)
    cid = (t + META_PAD) // CHUNK
    q = cid[META:, None]
    ok = (t[None, :] < META) | ((cid[None, :] >= 1) & (cid[None, :] >= q - 2) & (cid[None, :] <= q))
    m = np.where(ok, 0.0, NEG).reshape(2, P, TOK).transpose(1, 0, 2)
    return m.reshape(P, 2 * TOK)


def stack_parts(parts):
    at, where = 0, {}
    for name, a in parts:
        where[name] = (at, a.shape[1])
        at += a.shape[1]
    return np.concatenate([a.astype(np.float32) for _, a in parts], 1), where


class Lane:

    def __init__(self, sem):
        self.sem, self.done, self.steps, self.reached = sem, 0, [], {}

    def needs(self, after):
        flat, stack = {}, list(after)
        while stack:
            m = stack.pop()
            if m is None:
                continue
            if isinstance(m, list):
                stack.extend(m)
                continue
            s, v = m
            if v > self.reached.get(s, 0):
                flat[s] = max(flat.get(s, 0), v)
        self.reached.update(flat)
        return list(flat.items())

    def step(self, issue, after=()):
        self.done += 1
        self.steps.append((self.needs(after), issue, self.sem, 1))
        return (self.sem, self.done)

    def load(self, issue, arrival, after=()):
        arrival.count += 16
        self.steps.append((self.needs(after), issue, arrival.sem, 16))
        return (arrival.sem, arrival.count)

    def play(self, eng):
        for waits, issue, sem, n in self.steps:
            for s, v in waits:
                eng.wait_ge(s, v)
            if issue is not None:
                issue(eng).then_inc(sem, n)


class Arrival:

    def __init__(self, sem):
        self.sem, self.count = sem, 0


class Ring:

    def __init__(self, bufs):
        self.bufs, self.free, self.at = bufs, [[] for _ in bufs], 0

    def take(self):
        i = self.at % len(self.bufs)
        self.at += 1
        return i, self.bufs[i], self.free[i]


class Split:

    def __init__(self, hi, lo, chunks):
        self.hi, self.lo = hi, lo
        self.ready = [None] * chunks
        self.free = []

    def at(self, k, c0, n):
        return self.hi[:, k, c0:c0 + n], self.lo[:, k, c0:c0 + n]


class Joined:

    def __init__(self, a, b):
        self.a, self.b, self.cut = a, b, len(a.ready)

    @property
    def ready(self):
        return self.a.ready + self.b.ready

    def at(self, k, c0, n):
        return self.a.at(k, c0, n) if k < self.cut else self.b.at(k - self.cut, c0, n)


def program(nc, ins, out, where, ewhere):
    ctx = ExitStack()
    with ctx:
        def sem(name):
            return ctx.enter_context(nc.semaphore(name))

        def sb(name, shape, dt=F32, scope=ctx):
            return scope.enter_context(nc.sbuf_tensor(name, shape, dt))

        pe, act, dve, pool, sp = (Lane(sem(n)) for n in ("s_pe", "s_act", "s_dve", "s_pool", "s_sp"))

        h = sb("h", [P, KC, TOK])
        consts = sb("consts", [P, ins["consts"].shape[1]])
        cols = sb("cols", [P, ins["columns"].shape[1]])
        x_hi, x_lo = sb("x_hi", [P, KC, TOK], FR), sb("x_lo", [P, KC, TOK], FR)
        x = Split(x_hi, x_lo, KC)
        NRAW, NPART = 5, 4
        raw = [sb(f"w_raw{i}", [P, SLAB]) for i in range(NRAW)]
        w_hi = [sb(f"w_hi{i}", [P, SLAB], FR) for i in range(NPART)]
        w_lo = [sb(f"w_lo{i}", [P, SLAB], FR) for i in range(NPART)]
        squares = Ring([sb(f"square{i}", [P, TOK]) for i in range(3)])
        whole = Ring([sb(f"whole{i}", [P, TOK]) for i in range(3)])
        rstd = Ring([sb(f"rstd{i}", [P, TOK]) for i in range(2)])
        probs = Ring([sb(f"prob{i}", [P, 2 * SEQ]) for i in range(3)])
        probs_t = Ring([sb(f"prob_t{i}", [P, 3 * P]) for i in range(3)])
        stats = Ring([sb(f"stat{i}", [P, 8]) for i in range(6)])

        bank = [ctx.enter_context(nc.psum_tensor(f"bank{i}", [P, 512], F32)) for i in range(8)]
        acc = Ring(bank[0:3])
        score = Ring(bank[3:5])
        turned = Ring(bank[5:6])
        mixed = Ring(bank[6:7])
        sums = Ring(bank[7:8])

        w_sem = [Arrival(sem(f"s_w{i}")) for i in range(NRAW)]
        setup = Arrival(sem("s_setup"))
        tables = Arrival(sem("s_tables"))
        out_sem = Arrival(sem("s_out"))

        def const(name, c0=0, n=None):
            at, width = where[name]
            return consts[:, at + c0:at + (width if n is None else c0 + n)]

        def col(name, c=0, p0=0, pn=P):
            at = COLUMNS[name]
            return cols[p0:p0 + pn, at + c:at + c + 1]

        def activate(o, i, func, after, scale=1.0, bias=0.0, total=None):
            if total is None:
                return act.step(lambda e: e.activation(o, i, func, scale=scale, bias=bias), after)
            return act.step(lambda e: e.activation(o, i, func, scale=scale, bias=bias, accum_out=total), after)

        def copy_act(o, i, after):
            return act.step(lambda e: e.activation(o, i, ACT.Copy), after)

        def copy_dve(o, i, after):
            return dve.step(lambda e: e.tensor_copy(o, i), after)

        def pairwise(o, a, b, op, after, lane=dve):
            return lane.step(lambda e: e.tensor_tensor(o, a, b, op), after)

        def scaled(o, a, s1, op0, after, s2=None, op1=None):
            if op1 is None:
                return dve.step(lambda e: e.tensor_scalar(o, a, s1, None, op0), after)
            return dve.step(lambda e: e.tensor_scalar(o, a, s1, s2, op0, op1), after)

        def fused(o, a, s, b, op0, op1, after):
            return dve.step(lambda e: e.scalar_tensor_tensor(out=o, in0=a, scalar=s, in1=b, op0=op0, op1=op1), after)

        def reciprocal(o, a, after):
            return dve.step(lambda e: e.reciprocal(o, a), after)

        def product(o, pairs, after):
            def issue(e):
                for n, (lhsT, rhs) in enumerate(pairs):
                    mm = e.matmul(o, lhsT, rhs, start=(n == 0), stop=(n == len(pairs) - 1))
                return mm
            return pe.step(issue, after)

        loaded = []
        for dst, src in ((consts, ins["consts"]), (cols, ins["columns"])):
            loaded.append(sp.load(lambda e, d=dst, s=src: e.dma_start(d[:, :], s), setup))
        setup_ready = [loaded[-1]]
        x_loaded = sp.load(lambda e: e.dma_start(h[:, :, META:TOK], ins["x_t"].rearrange("p (c t) -> p c t", c=KC)), Arrival(sem("s_x")))
        meta_loaded = sp.load(lambda e: e.dma_start(h[:, :, 0:META], ins["meta_t"].rearrange("p (c t) -> p c t", c=KC)), Arrival(sem("s_meta")))
        h_ready = [x_loaded for _ in range(KC)]

        plan = []

        def tiles_plan(src, tiles, k):
            for t in tiles:
                for k0 in range(0, k // P, 8):
                    kn = min(8, k // P - k0)
                    plan.append((src[t][:, k0 * P:(k0 + kn) * P], kn * P))

        def rows_plan(src, n):
            per = SLAB // n
            for k0 in range(0, KC, per):
                kn = min(per, KC - k0)
                plan.append((src[:, k0 * n:(k0 + kn) * n], kn * n))

        for l in range(DEPTH):
            tiles_plan(ins["w_in"][l], range(0, 6), D)
            rows_plan(ins["w_moba_v"][l], MOBA_H * 64)
            tiles_plan(ins["w_in"][l], range(12, 16), D)
            rows_plan(ins["w_diff_v"][l], DIFF_H * 64)
            tiles_plan(ins["w_in"][l], range(20, 26), D)
            rows_plan(ins["w_sb_v"][l], SB_H * 64)
            tiles_plan(ins["w_in"][l], [9, 10, 11, 18, 19, 29, 30, 31], D)
            tiles_plan(ins["w_xk"][l], range(4), D)
            rows_plan(ins["w_xv"][l], 512)
            tiles_plan(ins["w_out"][l], range(8), D)
            tiles_plan(ins["w_xq"][l], range(4), D)
            tiles_plan(ins["w_xo"][l], range(8), 512)

        def ffn_plan(name, l):
            tiles_plan(ins[name + "_in"][l], range(2 * FT), D)
            tiles_plan(ins[name + "_out"][l], range(8), D_FF)

        ffn_plan("ffn1", 0)
        tiles_plan(ins["ev_in"], range(0, 5), D)
        plan.append((ins["ev_iw"], KC * IDX_H))
        tiles_plan(ins["ev_in"], range(5, 41), D)
        tiles_plan(ins["ev_out"], range(8), 1536)
        ffn_plan("ffn2", 0)
        ffn_plan("ffn1", 1)
        tiles_plan(ins["od_in"], range(10), D)
        tiles_plan(ins["od_out"], range(8), D)
        ffn_plan("ffn2", 1)

        converted = [None] * len(plan)
        raw_free = [[] for _ in range(NRAW)]
        part_free = [[] for _ in range(NPART)]
        landed = [None] * len(plan)
        state = {"use": 0, "fetch": 0, "convert": 0}

        def fetch():
            i = state["fetch"]
            if i >= len(plan):
                return
            src, width = plan[i]
            landed[i] = sp.load(lambda e: e.dma_start(raw[i % NRAW][:, 0:width], src), w_sem[i % NRAW], raw_free[i % NRAW])
            state["fetch"] += 1

        def convert():
            i = state["convert"]
            if i >= len(plan):
                return
            width = plan[i][1]
            w, hi, lo = raw[i % NRAW][:, 0:width], w_hi[i % NPART][:, 0:width], w_lo[i % NPART][:, 0:width]
            top = copy_act(hi, w, [landed[i], part_free[i % NPART]])
            rest = pairwise(lo, w, hi.bitcast(F32), ALU.subtract, [top])
            converted[i] = [top, rest]
            raw_free[i % NRAW] = [top, rest]
            state["convert"] += 1
            fetch()

        for _ in range(NRAW):
            fetch()
        for _ in range(NPART):
            convert()

        def slab(width):
            i = state["use"]
            assert plan[i][1] == width, (i, plan[i][1], width)
            state["use"] += 1
            return i, w_hi[i % NPART], w_lo[i % NPART], converted[i]

        def slab_done(i, mark):
            part_free[i % NPART] = [mark]
            convert()

        def three_products(e, o, w_h, w_l, a_h, a_l, first, last):
            e.matmul(o, w_h, a_h, start=first, stop=False)
            e.matmul(o, w_h, a_l, start=False, stop=False)
            return e.matmul(o, w_l, a_h, start=False, stop=last)

        def weight_tile(src, k, c0, n):
            b, o, free = acc.take()
            for k0 in range(0, k, 8):
                kn = min(8, k - k0)
                i, wh, wl, there = slab(kn * P)

                def issue(e, k0=k0, kn=kn, wh=wh, wl=wl):
                    for j in range(kn):
                        w = slice(j * P, (j + 1) * P)
                        mm = three_products(e, o[:, 0:n], wh[:, w], wl[:, w], *src.at(k0 + j, c0, n),
                                            k0 + j == 0, k0 + j == k - 1)
                    return mm
                mark = pe.step(issue, [there, free, src.ready[k0:k0 + kn]])
                slab_done(i, mark)
            return b, o, mark

        def weight_rows(src, n, blocks, c0=0):
            per = min(KC, SLAB // n)
            banks = [acc.take() for _ in blocks]
            for k0 in range(0, KC, per):
                kn = min(per, KC - k0)
                i, wh, wl, there = slab(kn * n)

                def issue(e, k0=k0, kn=kn, wh=wh, wl=wl):
                    for (t0, tn), (_, o, _) in zip(blocks, banks):
                        for j in range(kn):
                            w = slice(j * n, (j + 1) * n)
                            t = slice(c0 + t0, c0 + t0 + tn)
                            k = k0 + j
                            a_hi, a_lo = src.at(k, t.start, tn)
                            e.matmul(o[0:tn, 0:n], a_hi, wh[:, w], start=(k == 0), stop=False)
                            e.matmul(o[0:tn, 0:n], a_lo, wh[:, w], start=False, stop=False)
                            mm = e.matmul(o[0:tn, 0:n], a_hi, wl[:, w], start=False, stop=(k == KC - 1))
                    return mm
                mark = pe.step(issue, [there, [f for _, _, f in banks], src.ready[k0:k0 + kn]])
                slab_done(i, mark)
            return [(b, o) for b, o, _ in banks], mark

        later = []

        def flush():
            todo = list(later)
            later.clear()
            for f in todo:
                f()

        def split(y, y_mark, dst, k, c0, n, slot, after=()):
            hi, lo = dst.hi[:, k, c0:c0 + n], dst.lo[:, k, c0:c0 + n]
            top = copy_act(hi, y, [y_mark, dst.free, list(after)])
            rest = pairwise(lo, y, hi.bitcast(F32), ALU.subtract, [top])
            whole.free[slot] = [top, rest]
            dst.ready[k] = [top, rest]

        class Norm:

            def __init__(self, c0, n, chunks=KC, lhs="ones"):
                self.c0, self.n, self.chunks, self.at, self.lhs = c0, n, chunks, 0, lhs
                self.b = None

            def square(self, src, ready):
                if self.b is None:
                    self.b, self.o, self.free = sums.take()
                s, sq, free = squares.take()
                m = activate(sq[:, 0:self.n], src, ACT.Square, [ready, free])
                k = self.at
                self.at += 1

                def add():
                    mark = pe.step(lambda e: e.matmul(self.o[:, 0:self.n], const(self.lhs), sq[:, 0:self.n],
                                                      start=(k == 0), stop=(k == self.chunks - 1)),
                                   [m, self.free, setup_ready])
                    squares.free[s] = [mark]
                    self.mark = mark
                later.append(add)

            def finish(self, width):
                flush()
                r, rs, free = rstd.take()
                ln = activate(rs[:, 0:self.n], self.o[:, 0:self.n], ACT.Ln, [self.mark, free], scale=1.0 / width,
                              bias=const("eps"))
                sums.free[self.b] = [ln]
                m = activate(rs[:, 0:self.n], rs[:, 0:self.n], ACT.Exp, [ln], scale=-0.5)
                return r, rs, m

        def normalise(norm, gain, dst, ready, src=h):
            r, rs, m = norm.finish(D)
            for k in range(KC):
                s, y, free = whole.take()
                ym = fused(y[:, 0:norm.n], src[:, k, norm.c0:norm.c0 + norm.n], col(gain, k), rs[:, 0:norm.n],
                           ALU.mult, ALU.mult, [m, ready[k], free, setup_ready])
                split(y[:, 0:norm.n], ym, dst, k, norm.c0, norm.n, s)
            rstd.free[r] = [ym]

        def add_to_h(src, k, c0, n, factor=1.0, squares_for=None):
            for m in range(KC):
                b, o, mark = weight_tile(src, k, c0, n)
                flush()
                h_ready[m] = fused(h[:, m, c0:c0 + n], o[:, 0:n], factor, h[:, m, c0:c0 + n], ALU.mult, ALU.add,
                                   [mark, h_ready[m]])
                acc.free[b] = [h_ready[m]]
                if squares_for is not None:
                    squares_for.square(h[:, m, c0:c0 + n], h_ready[m])
            src.free = [mark]

        def weave(units, filler, active=3, per_round=1):
            waiting, running = list(units), []
            filling = True
            while waiting or running:
                if waiting and len(running) < active:
                    running.append(waiting.pop(0))
                still = []
                for u in running:
                    if next(u, None) is not None:
                        still.append(u)
                running = still
                for _ in range(per_round):
                    if filling and next(filler, None) is None:
                        filling = False
            while filling and next(filler, None) is not None:
                pass

        def turn_and_mix(p, p_mark, nq, kblocks, values, v_marks, place, write):
            t, tb, free = turned.take()

            def issue(e):
                for j, (k0, kn) in enumerate(kblocks):
                    mm = e.transpose(tb[0:kn, j * P:j * P + nq], p[0:nq, k0:k0 + kn], const("ident")[0:nq, 0:nq])
                return mm
            tm = pe.step(issue, [p_mark, free, setup_ready])
            s, pt, sfree = probs_t.take()
            full = len([1 for _, kn in kblocks if kn == P])
            marks = []
            if nq == P:
                marks.append(copy_act(pt[:, 0:full * P], tb[:, 0:full * P], [tm, sfree]))
            else:
                v3 = lambda a: a[:, 0:full * P].rearrange("p (j q) -> p j q", q=P)[:, :, 0:nq]
                marks.append(copy_act(v3(pt), v3(tb), [tm, sfree]))
            if full < len(kblocks):
                kn = kblocks[-1][1]
                marks.append(copy_act(pt[0:kn, full * P:full * P + nq], tb[0:kn, full * P:full * P + nq], [tm, sfree]))
            turned.free[t] = marks
            yield tm
            b, o, ofree = mixed.take()
            p0, pn = place
            pairs = [(values[j], pt[0:kn, j * P:j * P + nq]) for j, (_, kn) in enumerate(kblocks)]
            mm = product(o[p0:p0 + pn, 0:nq], pairs, [marks, ofree, v_marks])
            probs_t.free[s] = [mm]
            mixed.free[b] = [write(o[p0:p0 + pn, 0:nq], mm)]

        def attend(q, k, qk_marks, nq, nk, kblocks, bias, bias_marks, scale, values, v_marks, place, write, sink=None):
            b, o, free = score.take()
            sm = product(o[0:nq, 0:nk], [(q, k)], [qk_marks, free])
            pi, p, pfree = probs.take()
            si, st, sfree = stats.take()
            mx, shift, total, inv = (st[0:nq, c:c + 1] for c in (0, 1, 2, 3))
            if bias is None:
                m1 = dve.step(lambda e: e.tensor_reduce(mx, o[0:nq, 0:nk], AX.X, ALU.max), [sm, sfree])
                src, read = o[0:nq, 0:nk], [sm]
            else:
                m1 = dve.step(lambda e: e.tensor_tensor_reduce(p[0:nq, 0:nk], o[0:nq, 0:nk], bias, 1.0, GONE, ALU.add,
                                                               ALU.max, mx), [sm, pfree, sfree, bias_marks])
                src, read = p[0:nq, 0:nk], [m1]
            if sink is None:
                m2 = scaled(shift, mx, -scale, ALU.mult, [m1])
            else:
                m2 = scaled(mx, mx, scale, ALU.mult, [m1], sink, ALU.max)
                m2 = scaled(shift, mx, -1.0, ALU.mult, [m2])
            ex = activate(p[0:nq, 0:nk], src, ACT.Exp, [m2, read, pfree], scale=scale, bias=shift, total=total)
            score.free[b] = [ex if bias is None else m1]
            if sink is not None:
                es = activate(st[0:nq, 4:5], sink, ACT.Exp, [m2], bias=shift)
                ex = pairwise(total, total, st[0:nq, 4:5], ALU.add, [ex, es])
            m3 = reciprocal(inv, total, [ex])
            pm = scaled(p[0:nq, 0:nk], p[0:nq, 0:nk], inv, ALU.mult, [m3, ex])
            stats.free[si] = [pm]
            yield pm
            turn = turn_and_mix(p, pm, nq, kblocks, values, v_marks, place, write)
            probs.free[pi] = [next(turn)]
            yield True
            for _ in turn:
                pass

        scratch = {}

        def turned_tile(dst, ready, table, swap, c0, width):
            def gen(src):
                b, o, mark = weight_tile(src, KC, c0, width)
                flush()
                r, rq, free = scratch["raw"].take()
                m = copy_act(rq[:, 0:width], o[:, 0:width], [mark, free])
                acc.free[b] = [m]

                def rotate():
                    b2, o2, free2 = acc.take()
                    pm_ = product(o2[:, 0:width], [(const(swap), rq[:, 0:width])], [m, free2, setup_ready])
                    t_, tq, tfree = scratch["turn"].take()
                    a = pairwise(dst, rq[:, 0:width], table[0], ALU.mult, [m, table[2]], lane=pool)
                    c = pairwise(tq[:, 0:width], o2[:, 0:width], table[1], ALU.mult, [pm_, tfree, table[2]])
                    acc.free[b2] = [c]
                    d = pairwise(dst, dst, tq[:, 0:width], ALU.add, [a, c])
                    scratch["raw"].free[r] = [pm_, a]
                    scratch["turn"].free[t_] = [d]
                    ready.append(d)
                later.append(rotate)
            return gen

        def silu_tile(dst, ready, c0, n):
            def gen(src):
                b, o, mark = weight_tile(src, KC, c0, n)
                flush()
                m = activate(dst, o[:, 0:n], ACT.Exp, [mark], scale=-1.0)
                m = scaled(dst, dst, 1.0, ALU.add, [m])
                m = reciprocal(dst, dst, [m])
                m = pairwise(dst, dst, o[:, 0:n], ALU.mult, [m])
                acc.free[b] = [m]
                ready.append(m)
            return gen

        def plain_tile(dst, ready, c0, n):
            def gen(src):
                b, o, mark = weight_tile(src, KC, c0, n)
                flush()
                m = copy_act(dst, o[:, 0:n], [mark])
                acc.free[b] = [m]
                ready.append(m)
            return gen

        def rows_step(dst, ready, n, c0, blocks):
            def gen(src):
                banks, mark = weight_rows(src, n, blocks, c0)
                flush()
                for tb, (b, o) in enumerate(banks):
                    m = copy_act(dst[:, tb, :], o[:, 0:n], [mark])
                    acc.free[b] = [m]
                    ready.append(m)
            return gen

        def run(tiles, src):
            for t in tiles:
                t(src)
                yield True
            flush()


        def normed_tile(dst, ready, gain, c0, n):
            def gen(src):
                b, o, mark = weight_tile(src, KC, c0, n)
                flush()
                m = copy_act(dst, o[:, 0:n], [mark])
                acc.free[b] = [m]
                nm = Norm(0, n, 1, "pair")
                nm.square(dst, m)

                def scale():
                    r, rs, rm = nm.finish(64)
                    w = fused(dst, dst, col(gain), rs[:, 0:n], ALU.mult, ALU.mult, [rm])
                    rstd.free[r] = [w]
                    ready.append(w)
                later.append(scale)
            return gen

        def value_tile(dst, ready, f0):
            def gen(src):
                b, o, mark = weight_tile(src, KC, 0, TOK)
                flush()
                r, rv, free = scratch["raw"].take()
                m = copy_act(rv[:, 0:TOK], o[:, 0:TOK], [mark, free])
                acc.free[b] = [m]

                def turn():
                    t, tb, tfree = turned.take()

                    def issue(e):
                        for j, (k0, kn) in enumerate(KB2):
                            mm = e.transpose(tb[0:kn, j * P:(j + 1) * P], rv[:, k0:k0 + kn], const("ident"))
                        return mm
                    tm = pe.step(issue, [m, tfree, setup_ready])
                    scratch["raw"].free[r] = [tm]
                    w1 = copy_dve(dst[:, 0:2, f0:f0 + P], tb[:, 0:2 * P].rearrange("p (j f) -> p j f", j=2), [tm])
                    w2 = copy_dve(dst[0:16, 2, f0:f0 + P], tb[0:16, 2 * P:3 * P], [tm])
                    turned.free[t] = [w1, w2]
                    ready.extend([w1, w2])
                later.append(turn)
            return gen

        C0, N = META, SEQ
        QB = [(0, P), (P, P)]
        with ExitStack() as s1:
            sb1 = lambda name, shape, dt=F32: sb(name, shape, dt, s1)
            pos_i = sb1("pos_i", [P, SEQ], I32)
            pos = sb1("pos", [P, SEQ])
            angle, turns = sb1("angle", [P, SEQ]), sb1("turns", [P, SEQ])
            rope = {n: sb1("rope_" + n, [P, SEQ]) for n in ("cos64", "sin64", "cos32", "sin32")}
            scratch["raw"] = Ring([sb1(f"raw_qk{i}", [P, SEQ]) for i in range(2)])
            scratch["turn"] = Ring([sb1(f"turn_qk{i}", [P, SEQ]) for i in range(2)])
            mq, mk = sb1("moba_q", [P, MOBA_T, SEQ]), sb1("moba_k", [P, MOBA_T, SEQ])
            dq, dk = sb1("diff_q", [P, DIFF_T, SEQ]), sb1("diff_k", [P, DIFF_T, SEQ])
            sq_, sk = sb1("sb_q", [P, SB_T, SEQ]), sb1("sb_k", [P, SB_T, SEQ])
            mv, dv, sv = sb1("moba_v", [P, 2, 384]), sb1("diff_v", [P, 2, 256]), sb1("sb_v", [P, 2, 384])
            xk, xv = sb1("cross_k", [P, X_H, SEQ]), sb1("cross_v", [P, 2, 512])
            gate = sb1("gate", [P, 8, SEQ])
            mix = sb1("mix", [P, 8, SEQ])
            mem_t = sb1("mem_t", [P, KC, SEQ])
            m_hi, m_lo = sb1("mem_hi", [P, KC, SEQ], FR), sb1("mem_lo", [P, KC, SEQ], FR)
            memx = Split(m_hi, m_lo, KC)
            mem_rstd = sb1("mem_rstd", [P, SEQ])
            stick = Ring([sb1(f"stick{i}", [P, 3, 384]) for i in range(2)])
            lam_t = sb1("lam_t", [P, 8])
            lam_p = sb1("lam_p", [P, 2, 32])

            mem_loaded = sp.load(lambda e: e.dma_start(mem_t[:, :, :], ins["mem_t"].rearrange("p (c t) -> p c t", c=KC)),
                                 Arrival(sem("s_mem")))
            pos_loaded = sp.load(lambda e: e.dma_start(pos_i[:, :], ins["positions"].to_broadcast([P, SEQ])),
                                 Arrival(sem("s_pos")))

            pm = copy_dve(pos[:, :], pos_i[:, :], [pos_loaded])
            C1 = 6.28125
            C2 = float(np.float32(np.float64(int((2 * math.pi - C1) * 2 ** 21)) / 2 ** 21))
            C3 = float(np.float32(2 * math.pi - C1 - C2))
            MAGIC = 1.5 * 2 ** 23
            last = [pm, setup_ready]
            for inv, suffix in (("inv64", "64"), ("inv32", "32")):
                for name, quarter in (("cos", 0.25), ("sin", 0.0)):
                    a = scaled(angle[:, :], pos[:, :], const(inv), ALU.mult, [last])
                    t = scaled(turns[:, :], angle[:, :], 1.0 / (2 * math.pi), ALU.mult, [a], quarter, ALU.add)
                    t = scaled(turns[:, :], turns[:, :], MAGIC, ALU.add, [t])
                    t = scaled(turns[:, :], turns[:, :], -MAGIC, ALU.add, [t])
                    for c in (C1, C2, C3):
                        t = fused(angle[:, :], turns[:, :], -c, angle[:, :], ALU.mult, ALU.add, [t])
                    if quarter:
                        t = scaled(angle[:, :], angle[:, :], math.pi / 2, ALU.add, [t])
                    t = scaled(angle[:, :], angle[:, :], -3.1415925, ALU.max, [t], 3.1415925, ALU.min)
                    rope_mark = activate(rope[name + suffix][:, :], angle[:, :], ACT.Sin, [t])
                    last = [rope_mark]

            first = Norm(C0, N)
            for c in range(KC):
                first.square(h[:, c, C0:TOK], x_loaded)
                flush()
            norm = first
            lam = []
            for l in range(DEPTH):
                lam_init = 0.8 - 0.6 * math.exp(-0.3 * l)
                at = COLUMNS["lambda"] + l * 128
                m = None
                for j in range(2):
                    q1, k1 = cols[:, at + 64 * j:at + 64 * j + 32], cols[:, at + 64 * j + 32:at + 64 * j + 64]
                    m = pairwise(lam_p[:, j, :], q1, k1, ALU.mult, [setup_ready, m, lam])
                m = dve.step(lambda e, l=l: e.tensor_reduce(lam_t[:, 4 * l:4 * l + 2], lam_p[:, :, :], AX.X, ALU.add), [m])
                m = activate(lam_t[:, 4 * l:4 * l + 2], lam_t[:, 4 * l:4 * l + 2], ACT.Exp, [m])
                m = pairwise(lam_t[:, 4 * l + 2:4 * l + 3], lam_t[:, 4 * l + 1:4 * l + 2], lam_t[:, 4 * l:4 * l + 1],
                             ALU.subtract, [m])
                m = scaled(lam_t[:, 4 * l + 2:4 * l + 3], lam_t[:, 4 * l + 2:4 * l + 3], -lam_init, ALU.add, [m])
                lam = [scaled(lam_t[:, 4 * l + 3:4 * l + 4], col("head_gain", l), 1.0 - lam_init, ALU.mult, [m])]
            lam_ready = lam

            rd = [rope_mark]
            for l in range(DEPTH):
                normalise(norm, f"attn{l}", x, h_ready)
                r_mqk, r_mv, r_dqk, r_dv, r_sqk, r_sv, r_gate, r_xk, r_xv = ([] for _ in range(9))
                cs64 = (rope["cos64"][:, :], rope["sin64"][:, :], rd)
                cs32 = (rope["cos32"][:, :], rope["sin32"][:, :], rd)
                moba_tiles = [turned_tile(d[:, t, :], r_mqk, cs64, "swap64", C0, N) for d in (mq, mk) for t in range(MOBA_T)]
                moba_tiles.append(rows_step(mv, r_mv, MOBA_H * 64, C0, QB))
                diff_tiles = [turned_tile(d[:, t, :], r_dqk, cs32, "swap32", C0, N) for d in (dq, dk) for t in range(DIFF_T)]
                diff_tiles.append(rows_step(dv, r_dv, DIFF_H * 64, C0, QB))
                sb_tiles = [plain_tile(d[:, t, :], r_sqk, C0, N) for d in (sq_, sk) for t in range(SB_T)]
                sb_tiles.append(rows_step(sv, r_sv, SB_H * 64, C0, QB))
                gate_tiles = [silu_tile(gate[:, t, :], r_gate, C0, N) for t in range(8)]
                for _ in run(moba_tiles, x):
                    pass

                mixed_marks = [[] for _ in range(8)]

                def moba_unit(hd, qb):
                    t, p0 = hd // 2, (hd % 2) * 64
                    nk = P * (qb + 1)

                    def write(o, m):
                        w = copy_act(mix[p0:p0 + 64, t, qb * P:(qb + 1) * P], o, [m])
                        mixed_marks[t].append(w)
                        return w
                    return attend(mq[p0:p0 + 64, t, qb * P:(qb + 1) * P], mk[p0:p0 + 64, t, 0:nk], r_mqk, P, nk,
                                  QB[:qb + 1], const("causal", P * (1 - qb), nk), setup_ready, 64 ** -0.5,
                                  [mv[:, j, hd * 64:(hd + 1) * 64] for j in range(qb + 1)], r_mv, (p0, 64), write)

                def diff_unit(hd, qb, l=l):
                    nk = P * (qb + 1)
                    scale = 32 ** -0.5
                    t = hd // 2
                    b, o, free = score.take()
                    pi, p, pfree = probs.take()
                    si, st, sfree = stats.take()
                    sc = []
                    for c in range(2):
                        p0 = ((2 * hd + c) % 4) * 32
                        sc.append(product(o[:, c * nk:(c + 1) * nk],
                                          [(dq[p0:p0 + 32, t, qb * P:(qb + 1) * P], dk[p0:p0 + 32, t, 0:nk])],
                                          [r_dqk, free, list(sc)]))
                    ms = []
                    for c in range(2):
                        ms.append(dve.step(lambda e, c=c: e.tensor_tensor_reduce(
                            p[:, c * nk:(c + 1) * nk], o[:, c * nk:(c + 1) * nk], const("causal", P * (1 - qb), nk), 1.0,
                            GONE, ALU.add, ALU.max, st[:, c:c + 1]), [sc[1], pfree, sfree, setup_ready]))
                    score.free[b] = [ms[1]]
                    m2 = scaled(st[:, 2:4], st[:, 0:2], -scale, ALU.mult, ms)
                    ex = [activate(p[:, c * nk:(c + 1) * nk], p[:, c * nk:(c + 1) * nk], ACT.Exp, [m2], scale=scale,
                                   bias=st[:, 2 + c:3 + c], total=st[:, 4 + c:5 + c]) for c in range(2)]
                    m3 = reciprocal(st[:, 6:8], st[:, 4:6], ex)
                    m4 = scaled(st[:, 7:8], st[:, 7:8], lam_t[:, 4 * l + 2:4 * l + 3], ALU.mult, [m3, lam_ready])
                    m5 = scaled(p[:, 0:nk], p[:, 0:nk], st[:, 6:7], ALU.mult, [m3])
                    pm_ = fused(p[:, 0:nk], p[:, nk:2 * nk], st[:, 7:8], p[:, 0:nk], ALU.mult, ALU.add, [m4, m5])
                    stats.free[si] = [pm_]
                    yield pm_

                    def write(o_, m):
                        w = copy_act(mix[(hd % 2) * 64:(hd % 2) * 64 + 64, MOBA_T + t, qb * P:(qb + 1) * P], o_, [m])
                        mixed_marks[MOBA_T + t].append(w)
                        return w
                    turn = turn_and_mix(p, pm_, P, QB[:qb + 1], [dv[:, j, hd * 64:(hd + 1) * 64] for j in range(qb + 1)],
                                        r_dv, ((hd % 2) * 64, 64), write)
                    probs.free[pi] = [next(turn)]
                    yield True
                    for _ in turn:
                        pass

                def diff_norm(t, l=l):
                    tile = mix[:, MOBA_T + t, :]
                    nm = Norm(0, SEQ, 1, "pair")
                    nm.square(tile, mixed_marks[MOBA_T + t])
                    yield True
                    r, rs, m = nm.finish(64)
                    w = fused(tile, tile, lam_t[:, 4 * l + 3:4 * l + 4], rs[:, 0:SEQ], ALU.mult, ALU.mult, [m, lam_ready])
                    rstd.free[r] = [w]
                    mixed_marks[MOBA_T + t].append(w)

                def stick_unit(hd):
                    t, p0 = hd // 2, (hd % 2) * 64
                    scale = 64 ** -0.5
                    q, k = sq_[p0:p0 + 64, t, :], sk[p0:p0 + 64, t, :]
                    si, st, sfree = stick.take()
                    b, o, free = score.take()
                    z0 = product(o[:, 0:256], [(k[:, 0:P], q)], [r_sqk, free])
                    z1 = product(o[:, 256:384], [(k[:, P:], q[:, P:])], [z0])
                    z = o[:, 0:384]
                    soft, log_beta, log_rest = st[:, 0, :], st[:, 1, :], st[:, 2, :]
                    mag = activate(soft, z, ACT.Abs, [z1, sfree], scale=scale)
                    m = activate(soft, soft, ACT.Exp, [mag], scale=-1.0)
                    m = activate(soft, soft, ACT.Ln, [m], bias=1.0)
                    lb = scaled(log_beta, z, scale, ALU.mult, [mag, sfree], 0.0, ALU.min)
                    lb = pairwise(log_beta, log_beta, soft, ALU.subtract, [m, lb])
                    lr = fused(log_rest, z, -scale, log_beta, ALU.mult, ALU.add, [lb])
                    score.free[b] = [lr]
                    lr = pairwise(log_rest, log_rest, const("sb"), ALU.mult, [lr, setup_ready])
                    yield True
                    b2, o2, free2 = score.take()

                    def between(e):
                        e.matmul(o2[:, 0:256], const("later"), log_rest[:, 0:256], start=True, stop=False)
                        e.matmul(o2[:, P:256], const("ones"), log_rest[:, 256:384], start=False, stop=True)
                        return e.matmul(o2[:, 256:384], const("later"), log_rest[:, 256:384], start=True, stop=True)
                    bm = pe.step(between, [lr, free2, setup_ready])
                    w = pairwise(soft, o2[:, 0:384], log_beta, ALU.add, [bm, lb, m])
                    score.free[b2] = [w]
                    w = activate(soft, soft, ACT.Exp, [w])
                    w = pairwise(soft, soft, const("sb"), ALU.mult, [w, setup_ready])
                    yield True
                    b3, o3, free3 = mixed.take()

                    def values(e):
                        e.matmul(o3[p0:p0 + 64, 0:256], sv[:, 0, hd * 64:(hd + 1) * 64], soft[:, 0:256], start=True, stop=False)
                        return e.matmul(o3[p0:p0 + 64, P:256], sv[:, 1, hd * 64:(hd + 1) * 64], soft[:, 256:384],
                                        start=False, stop=True)
                    vm = pe.step(values, [w, free3, r_sv])
                    stick.free[si] = [vm]
                    wr = copy_act(mix[p0:p0 + 64, MOBA_T + DIFF_T + t, :], o3[p0:p0 + 64, 0:256], [vm])
                    mixed.free[b3] = [wr]
                    mixed_marks[MOBA_T + DIFF_T + t].append(wr)

                def mem_filler(l=l):
                    if l == 0:
                        flush()
                        mem_norm = Norm(0, SEQ)
                        for c in range(KC):
                            mem_norm.square(mem_t[:, c, :], mem_loaded)
                            flush()
                        ln = activate(mem_rstd[:, :], mem_norm.o[:, 0:SEQ], ACT.Ln, [mem_norm.mark], scale=1.0 / D,
                                      bias=const("eps"))
                        sums.free[mem_norm.b] = [ln]
                        mem_filler.rstd = activate(mem_rstd[:, :], mem_rstd[:, :], ACT.Exp, [ln], scale=-0.5)
                    for k in range(KC):
                        s, y, free = whole.take()
                        ym = fused(y[:, 0:SEQ], mem_t[:, k, :], col(f"memg{l}", k), mem_rstd[:, :], ALU.mult, ALU.mult,
                                   [mem_marks[0], free, setup_ready] if l else [mem_filler.rstd, free, setup_ready])
                        split(y[:, 0:SEQ], ym, memx, k, 0, SEQ, s)
                    mem_marks[0] = ym
                    yield True
                    for t in range(X_H):
                        plain_tile(xk[:, t, :], r_xk, 0, SEQ)(memx)
                        yield True
                    rows_step(xv, r_xv, 512, 0, QB)(memx)
                    memx.free = [r_xv[-1]]
                    yield True

                mem_marks = [None] if l == 0 else mem_marks

                def chain(*gens):
                    for g in gens:
                        for v in g:
                            yield v

                units = [moba_unit(hd, qb) for hd in range(MOBA_H) for qb in range(2)]
                weave(units, run(diff_tiles, x))
                units = [u for t in range(DIFF_T) for u in
                         [diff_unit(hd, qb) for hd in (2 * t, 2 * t + 1) for qb in range(2)]]
                weave(units, run(sb_tiles, x))
                units = [stick_unit(hd) for hd in range(SB_H)] + [diff_norm(t) for t in range(DIFF_T)]
                weave(units, chain(run(gate_tiles, x), mem_filler()), active=2)
                flush()
                x.free = [r_gate[-1]]
                for t in range(8):
                    s, y, free = whole.take()
                    ym = pairwise(y[:, 0:N], mix[:, t, :], gate[:, t, :], ALU.mult, [mixed_marks[t], r_gate, free])
                    split(y[:, 0:N], ym, x, t, C0, N, s)
                norm = Norm(C0, N)
                add_to_h(x, KC, C0, N, squares_for=norm)

                normalise(norm, f"xattn{l}", x, h_ready)
                r_q = []
                for _ in run([plain_tile(mq[:, t, :] if t < 3 else mk[:, 0, :], r_q, C0, N) for t in range(X_H)], x):
                    pass
                x.free = [r_q[-1]]
                cross_marks = [[] for _ in range(X_H)]

                def cross_unit(hd, qb):
                    q = (mq[:, hd, :] if hd < 3 else mk[:, 0, :])[:, qb * P:(qb + 1) * P]

                    def write(o, m):
                        w = copy_act(mix[:, hd, qb * P:(qb + 1) * P], o, [m])
                        cross_marks[hd].append(w)
                        if qb == 1:
                            s, y, free = whole.take()
                            ym = copy_dve(y[:, 0:N], mix[:, hd, :], [cross_marks[hd], free])
                            split(y[:, 0:N], ym, x, hd, C0, N, s)
                        return w
                    return attend(q, xk[:, hd, :], [r_q, r_xk], P, SEQ, QB, None, None, 128 ** -0.5,
                                  [xv[:, j, hd * P:(hd + 1) * P] for j in range(2)], r_xv, (0, P), write)
                weave([cross_unit(hd, qb) for hd in range(X_H) for qb in range(2)], iter(()))
                norm = Norm(C0, N)
                add_to_h(x, 4, C0, N, squares_for=norm)

            r, rs, m = norm.finish(D)
            for k in range(KC):
                h_ready[k] = fused(h[:, k, C0:TOK], h[:, k, C0:TOK], col("final", k), rs[:, 0:N], ALU.mult, ALU.mult,
                                   [m, h_ready[k]])
            rstd.free[r] = [h_ready[KC - 1]]

        def ffn(l, gain, norm, c0, n, squares_for, tag):
            with ExitStack() as s2:
                gated = Ring([sb(f"{tag}_gated{i}", [P, TOK], F32, s2) for i in range(3)])
                a = Split(sb(tag + "_hi", [P, FT, TOK], FR, s2), sb(tag + "_lo", [P, FT, TOK], FR, s2), FT)
                normalise(norm, gain, x, h_ready)
                for j in range(FT):
                    b, o, mark = weight_tile(x, KC, c0, n)
                    g, gt, free = gated.take()
                    gm = activate(gt[:, 0:n], o[:, 0:n], ACT.Silu, [mark, free])
                    acc.free[b] = [gm]
                    b, o, mark = weight_tile(x, KC, c0, n)
                    s, y, free = whole.take()
                    ym = pairwise(y[:, 0:n], o[:, 0:n], gt[:, 0:n], ALU.mult, [mark, gm, free])
                    acc.free[b], gated.free[g] = [ym], [ym]
                    split(y[:, 0:n], ym, a, j, c0, n, s)
                x.free = [mark]
                add_to_h(a, FT, c0, n, 0.5, squares_for)

        def even_mixer(norm, squares_for):
            with ExitStack() as s2:
                sb2 = lambda name, shape, dt=F32: sb("ev_" + name, shape, dt, s2)
                even, decay = sb2("tables", [P, ins["even"].shape[1]]), sb2("decay", [P, B_H, 432])
                aq, ak, iq, bq, bk = (sb2(n, [P, 4, TOK]) for n in ("aq", "ak", "iq", "bq", "bk"))
                ik, iw = sb2("ik", [P, TOK]), sb2("iw", [P, 3, IDX_H])
                av, bv, bg = sb2("av", [P, 3, 512]), sb2("bv", [P, 3, 1024]), sb2("bg", [P, 8, TOK])
                rest, bias = sb2("rest", [P, 3, TOK]), sb2("bias", [P, 3, TOK])
                best = Ring([sb2(f"best{i}", [P, 8]) for i in range(3)])
                scratch["raw"] = Ring([sb2(f"raw{i}", [P, TOK]) for i in range(2)])
                scratch["turn"] = Ring([sb2(f"turn{i}", [P, TOK]) for i in range(2)])
                ya = sb2("ya", [P, 4, TOK])
                yas = Split(sb2("ya_hi", [P, 4, TOK], FR), sb2("ya_lo", [P, 4, TOK], FR), 4)
                yb = Ring([sb2(f"yb{i}", [P, TOK]) for i in range(2)])
                tm = [sp.load(lambda e: e.dma_start(even[:, :], ins["even"]), tables, [h_ready[KC - 1]]),
                      sp.load(lambda e: e.dma_start(decay[:, :, :], ins["decay"].rearrange("p (h n) -> p h n", h=B_H)), tables)]
                tm = [tm[1]]

                def table(name, c0=0, n=None):
                    at, width = ewhere[name]
                    return even[:, at + c0:at + (width if n is None else c0 + n)]

                normalise(norm, "mixg0", x, h_ready)
                r_i, r_iw, r_a, r_av, r_b, r_bv, r_bg = ([] for _ in range(7))
                for _ in run([plain_tile(iq[:, t, :], r_i, 0, TOK) for t in range(4)] + [plain_tile(ik[:, :], r_i, 0, TOK)], x):
                    pass
                banks, mark = weight_rows(x, IDX_H, KB2)
                for (t0, tn), (b, o), j in zip(KB2, banks, range(3)):
                    m = scaled(iw[0:tn, j, :], o[0:tn, 0:IDX_H], IDX_H ** -0.5 * 64 ** -0.5, ALU.mult, [mark])
                    acc.free[b] = [m]
                    r_iw.append(m)
                rq = (table("cosq"), table("sinq"), tm)
                rk = (table("cosk"), table("sink"), tm)
                tiles = [normed_tile(aq[:, t, :], r_a, "a_q", 0, TOK) for t in range(4)]
                tiles += [normed_tile(ak[:, t, :], r_a, "a_k", 0, TOK) for t in range(4)]
                tiles += [value_tile(av, r_av, t * P) for t in range(4)]
                tiles += [turned_tile(bq[:, t, :], r_b, rq, "swapr", 0, TOK) for t in range(4)]
                tiles += [turned_tile(bk[:, t, :], r_b, rk, "swapr", 0, TOK) for t in range(4)]
                tiles += [value_tile(bv, r_bv, t * P) for t in range(8)]
                tiles += [silu_tile(bg[:, t, :], r_bg, 0, TOK) for t in range(8)]
                bias_ready = [None] * 3
                width = [144, TOK, TOK]
                blocks = [[(0, P), (P, 16)], KB2, KB2]

                def index_unit(qb):
                    (q0, nq), nk = KB2[qb], width[qb]
                    adm = table("adm", qb * TOK, nk)[0:nq, :]
                    left = rest[0:nq, qb, 0:nk]
                    m = None
                    for hd in range(IDX_H):
                        t, p0 = hd // 2, (hd % 2) * 64
                        b, o, free = score.take()
                        sm = product(o[0:nq, 0:nk], [(iq[p0:p0 + 64, t, q0:q0 + nq], ik[p0:p0 + 64, 0:nk])], [r_i, free])
                        pi, p, pfree = probs.take()
                        rm = activate(p[0:nq, 0:nk], o[0:nq, 0:nk], ACT.Relu, [sm, pfree])
                        score.free[b] = [rm]
                        m = fused(left, p[0:nq, 0:nk], iw[0:nq, qb, hd:hd + 1], left if hd else adm, ALU.mult, ALU.add,
                                  [rm, m, r_iw, tm])
                        probs.free[pi] = [m]
                        if hd % 2:
                            yield True
                    for _ in range(TOP_K // 8):
                        bi, top, bfree = best.take()
                        m = dve.step(lambda e, top=top: e.max(top[0:nq, :], left), [m, bfree])
                        m = dve.step(lambda e, top=top: e.match_replace(left, top[0:nq, :], left, GONE), [m])
                        best.free[bi] = [m]
                        yield True
                    m = scaled(bias[0:nq, qb, 0:nk], left, 0.5 * GONE, ALU.is_gt, [m], NEG, ALU.mult)
                    bias_ready[qb] = pairwise(bias[0:nq, qb, 0:nk], bias[0:nq, qb, 0:nk], adm, ALU.add, [m])

                weave([index_unit(qb) for qb in range(3)], run(tiles, x))
                x.free = [r_bg[-1]]

                ya_marks = [[] for _ in range(4)]

                def sparse_unit(hd, qb):
                    (q0, nq), nk = KB2[qb], width[qb]
                    t, p0 = hd // 2, (hd % 2) * 64

                    def write(o, m):
                        w = copy_act(ya[p0:p0 + 64, t, q0:q0 + nq], o, [m])
                        ya_marks[t].append(w)
                        if len(ya_marks[t]) == 6:
                            s, y, free = whole.take()
                            ym = copy_dve(y[:, :], ya[:, t, :], [ya_marks[t], free])
                            split(y[:, :], ym, yas, t, 0, TOK, s)
                        return w
                    return attend(aq[p0:p0 + 64, t, q0:q0 + nq], ak[p0:p0 + 64, t, 0:nk], r_a, nq, nk, blocks[qb],
                                  bias[0:nq, qb, 0:nk], bias_ready[qb], 64 ** -0.5,
                                  [av[0:kn, j, hd * 64:(hd + 1) * 64] for j, (_, kn) in enumerate(blocks[qb])],
                                  r_av, (p0, 64), write)

                def retention_unit(hd):
                    t, p0 = hd // 2, (hd % 2) * 64
                    q, k = bq[p0:p0 + 64, t, :], bk[p0:p0 + 64, t, :]
                    b, o, free = score.take()

                    def scores(e):
                        at = 0
                        for k0, kn in KB2:
                            mm = e.matmul(o[0:kn, at:at + TOK - k0], k[:, k0:k0 + kn], q[:, k0:TOK], start=True, stop=True)
                            at += TOK - k0
                        return mm
                    sm = pe.step(scores, [r_b, free])
                    pi, p, pfree = probs.take()
                    m1 = pairwise(p[:, 0:416], o[:, 0:416], decay[:, hd, 0:416], ALU.mult, [sm, pfree, tm])
                    m2 = pairwise(p[0:16, 416:432], o[0:16, 416:432], decay[0:16, hd, 416:432], ALU.mult, [sm, pfree, tm])
                    score.free[b] = [m1, m2]
                    yield True
                    b2, mx, free2 = mixed.take()

                    def values(e):
                        at = 0
                        for j, (k0, kn) in enumerate(KB2):
                            mm = e.matmul(mx[:, k0:TOK], bv[0:kn, j, hd * P:(hd + 1) * P], p[0:kn, at:at + TOK - k0],
                                          start=(j == 0), stop=(j == 2))
                            at += TOK - k0
                        return mm
                    vm = pe.step(values, [m1, m2, free2, r_bv])
                    probs.free[pi] = [vm]
                    yi, y, yfree = yb.take()
                    ym = copy_act(y[:, :], mx[:, 0:TOK], [vm, yfree])
                    mixed.free[b2] = [ym]
                    yield True
                    nm = Norm(0, TOK, 1, "ones")
                    nm.square(y[:, :], ym)
                    flush()
                    r, rs, rm = nm.finish(P)
                    s, z, zfree = whole.take()
                    m = pairwise(z[:, :], y[:, :], rs[:, :], ALU.mult, [rm, zfree])
                    rstd.free[r], yb.free[yi] = [m], [m]
                    m = pairwise(z[:, :], z[:, :], bg[:, hd, :], ALU.mult, [m, r_bg])
                    split(z[:, :], m, x, hd, 0, TOK, s)

                units = [sparse_unit(hd, qb) for hd in range(A_H) for qb in range(3)]
                for hd in range(B_H):
                    units.insert(4 * hd + 1, retention_unit(hd))
                weave(units, iter(()))
                add_to_h(Joined(yas, x), 12, 0, TOK, squares_for=squares_for)
                x.free = [(pe.sem, pe.done)]

        def odd_mixer(norm, squares_for):
            with ExitStack() as s2:
                sb2 = lambda name, shape, dt=F32: sb("od_" + name, shape, dt, s2)
                window, dmix = sb2("window", [P, 2, TOK]), sb2("mix", [P, 512])
                cq, ck, cv = sb2("cq", [P, 4, TOK]), sb2("ck", [P, TOK]), sb2("cv", [P, 3, P])
                scratch["raw"] = Ring([sb2(f"raw{i}", [P, TOK]) for i in range(2)])
                runs = Ring([sb2(f"run{i}", [P, 2, TOK]) for i in range(2)])
                pooled = Ring([sb2(f"pooled{i}", [P, SEQ]) for i in range(2)])
                yc = sb2("yc", [P, 4, SEQ])
                ycs = Split(sb2("yc_hi", [P, 4, TOK], FR), sb2("yc_lo", [P, 4, TOK], FR), 4)
                yds = Split(sb2("yd_hi", [P, 4, TOK], FR), sb2("yd_lo", [P, 4, TOK], FR), 4)
                tm = [sp.load(lambda e: e.dma_start(window[:, :, :], ins["window"].rearrange("p (b n) -> p b n", b=2)), tables,
                              [h_ready[KC - 1]]),
                      sp.load(lambda e: e.dma_start(dmix[:, :], ins["od_mix"]), tables)]
                tm = [tm[1]]
                normalise(norm, "mixg1", x, h_ready)
                r_c, r_cv = [], []

                def pool_tile(g):
                    def gen(src):
                        b, o, mark = weight_tile(src, KC, 0, TOK)
                        flush()
                        r, rv, free = scratch["raw"].take()
                        m = copy_act(rv[:, :], o[:, 0:TOK], [mark, free])
                        raw_m = m
                        acc.free[b] = [m]
                        u, ru, ufree = runs.take()
                        have = rv[:, :]
                        for step in range(g + 1):
                            w, lo = 1 << step, (2 << step) - 1
                            to = ru[:, step % 2, :]
                            m = pairwise(to[:, lo:], have[:, lo:], have[:, lo - w:TOK - w], ALU.add, [m, ufree])
                            have = to
                        q, py, pfree = pooled.take()
                        m = fused(py[:, :], have[:, META:], 1.0 / (2 << g), rv[:, META:], ALU.mult, ALU.subtract, [m, pfree])
                        runs.free[u], scratch["raw"].free[r] = [m], [m]

                        def mix_groups():
                            b2, o2, free2 = acc.take()
                            mm = product(o2[:, 0:SEQ], [(dmix[:, g * P:(g + 1) * P], py[:, :])], [m, free2, tm])
                            pooled.free[q] = [mm]
                            s, y, sfree = whole.take()
                            ym = scaled(y[:, 0:SEQ], o2[:, 0:SEQ], col("d_scale", g), ALU.mult, [mm, sfree])
                            acc.free[b2] = [ym]
                            split(y[:, 0:SEQ], ym, yds, g, META, SEQ, s)
                        later.append(mix_groups)
                    return gen

                tiles = [normed_tile(cq[:, t, :], r_c, "c_q", 0, TOK) for t in range(4)]
                tiles += [normed_tile(ck[:, :], r_c, "c_k", 0, TOK), value_tile(cv, r_cv, 0)]
                for _ in run(tiles, x):
                    pass
                yc_marks = [[] for _ in range(4)]

                def window_unit(j, half, qb):
                    p0, nk = half * 64, [144, TOK][qb]
                    blocks = [[(0, P), (P, 16)], KB2][qb]

                    def write(o, m):
                        w = copy_act(yc[p0:p0 + 64, j, qb * P:(qb + 1) * P], o, [m])
                        yc_marks[j].append(w)
                        if len(yc_marks[j]) == 4:
                            s, y, free = whole.take()
                            ym = copy_dve(y[:, 0:SEQ], yc[:, j, :], [yc_marks[j], free])
                            split(y[:, 0:SEQ], ym, ycs, j, META, SEQ, s)
                        return w
                    return attend(cq[p0:p0 + 64, j, META + qb * P:META + (qb + 1) * P], ck[p0:p0 + 64, 0:nk], r_c, P, nk,
                                  blocks, window[:, qb, 0:nk], tm, 64 ** -0.5,
                                  [cv[0:kn, i, p0:p0 + 64] for i, (_, kn) in enumerate(blocks)], r_cv, (p0, 64), write,
                                  sink=col("sinks", half * 4 + j))

                weave([window_unit(j, half, qb) for j in range(4) for half in range(2) for qb in range(2)],
                      run([pool_tile(g) for g in range(4)], x))
                x.free = [(pe.sem, pe.done)]
                add_to_h(Joined(ycs, yds), KC, META, SEQ, squares_for=squares_for)

        norm = Norm(0, TOK)
        for c in range(KC):
            h_ready[c] = [h_ready[c], meta_loaded]
            norm.square(h[:, c, :], h_ready[c])
            flush()
        for_mix0, for_ffn20, for_ffn11, for_mix1, for_ffn21 = (Norm(*c) for c in 4 * [(0, TOK)] + [(META, SEQ)])
        ffn(0, "f1g0", norm, 0, TOK, for_mix0, "ffn10")
        even_mixer(for_mix0, for_ffn20)
        ffn(0, "f2g0", for_ffn20, 0, TOK, for_ffn11, "ffn20")
        ffn(1, "f1g1", for_ffn11, 0, TOK, for_mix1, "ffn11")
        odd_mixer(for_mix1, for_ffn21)
        ffn(1, "f2g1", for_ffn21, META, SEQ, None, "ffn21")
        out_v = out.rearrange("p (c t) -> p c t", c=KC)
        for c in range(KC):
            sp.load(lambda e, c=c: e.dma_start(out_v[:, c, :], h[:, c, META:TOK]), out_sem, [h_ready[c]])
        sp.steps.append(([(out_sem.sem, out_sem.count)], None, None, 0))

        block = ctx.enter_context(nc.Block())

        block.sync(sp.play)
        block.scalar(act.play)
        block.vector(dve.play)
        block.gpsimd(pool.play)
        block.tensor(pe.play)


COLUMNS = {}


def column_layout():
    at = 0
    for name, width in ([(f"{n}{l}", KC) for n in ("attn", "xattn", "memg", "f1g", "mixg", "f2g") for l in range(DEPTH)]
                        + [("final", KC), ("head_gain", DEPTH), ("a_q", 1), ("a_k", 1), ("c_q", 1), ("c_k", 1),
                           ("sinks", C_H), ("d_scale", 4), ("lambda", DEPTH * 128)]):
        COLUMNS[name] = at
        at += width
    return at


N_COLUMNS = column_layout()


def pack_tiles(w):
    lead, (k, n) = w.shape[:-2], w.shape[-2:]
    a = w.reshape(*lead, k // P, P, n // P, P)
    j = len(lead)
    return np.ascontiguousarray(a.transpose(*range(j), j + 2, j + 1, j, j + 3)).reshape(*lead, n // P, P, k)


def pack_rows(w):
    lead, (k, n) = w.shape[:-2], w.shape[-2:]
    j = len(lead)
    a = w.reshape(*lead, k // P, P, n).transpose(*range(j), j + 1, j, j + 2)
    return np.ascontiguousarray(a).reshape(*lead, P, (k // P) * n)


def feature_major(a):
    return np.ascontiguousarray(a.T.reshape(-1, P, a.shape[0]).transpose(1, 0, 2)).reshape(P, -1)


def per_partition(v):
    return v.reshape(-1, P).T


def everywhere(v):
    return np.broadcast_to(v.reshape(1, -1), (P, v.size))


def layouts(a):
    w_in = a["w_in"]
    d = {}
    d["x_t"] = feature_major(a["x"][0])
    d["mem_t"] = feature_major(a["mem"][0])
    d["meta_t"] = feature_major(a["meta_tokens_2"])
    d["positions"] = np.ascontiguousarray(a["positions"])
    twice = lambda v: np.concatenate([v, v]).reshape(P, 1)
    columns = [per_partition(a[n][l]) for n in ("attn_norm_g", "xattn_norm_g", "mem_norm_g", "ffn1_norm_2",
                                                 "mix_norm_2", "ffn2_norm_2") for l in range(DEPTH)]
    columns += [per_partition(a["final_norm_g"])]
    columns += [twice(a["diff_head_norm_g"][l]) for l in range(DEPTH)]
    columns += [twice(a[n][0]) for n in ("ev_a_q_norm_2", "ev_a_k_norm_2", "od_c_q_norm_2", "od_c_k_norm_2")]
    columns += [everywhere(a["od_c_sinks_2"][0]), per_partition(a["od_d_scale_2"][0])]
    for l in range(DEPTH):
        columns += [everywhere(a[n][l]) for n in ("diff_lambda_q1", "diff_lambda_k1", "diff_lambda_q2", "diff_lambda_k2")]
    d["columns"] = np.ascontiguousarray(np.concatenate(columns, 1))
    assert d["columns"].shape[1] == N_COLUMNS
    d["w_in"] = pack_tiles(w_in)
    d["w_moba_v"] = pack_rows(w_in[:, :, 768:1152])
    d["w_diff_v"] = pack_rows(w_in[:, :, 2048:2304])
    d["w_sb_v"] = pack_rows(w_in[:, :, 3328:3712])
    d["w_out"] = pack_tiles(a["w_out"])
    d["w_xq"] = pack_tiles(a["w_xq"])
    d["w_xk"] = pack_tiles(a["w_xkv"][:, :, :512])
    d["w_xv"] = pack_rows(a["w_xkv"][:, :, 512:])
    d["w_xo"] = pack_tiles(a["w_xo"])
    for f in ("ffn1", "ffn2"):
        w = a[f + "_w_in_2"].reshape(DEPTH, D, 2, FT, P).transpose(0, 1, 3, 2, 4).reshape(DEPTH, D, 2 * D_FF)
        d[f + "_in"] = pack_tiles(w)
        d[f + "_out"] = pack_tiles(a[f + "_w_out_2"])
    ev = a["ev_w_in_2"][0]
    ik = ev[:, 2048:2112]
    d["ev_in"] = pack_tiles(np.concatenate([ev[:, 1536:2048], ik, ik, ev[:, 0:1536], ev[:, 2120:5192]], 1))
    d["ev_iw"] = pack_rows(ev[:, 2112:2120])
    d["ev_out"] = pack_tiles(a["ev_w_out_2"][0])
    od = a["od_w_in_2"][0]
    cq = od[:, 0:512].reshape(D, 2, 4, 64).transpose(0, 2, 1, 3).reshape(D, 512)
    d["od_in"] = pack_tiles(np.concatenate([cq, od[:, 512:1280]], 1))
    od_out = a["od_w_out_2"][0]
    co = od_out[0:512].reshape(2, 4, 64, D).transpose(1, 0, 2, 3).reshape(512, D)
    d["od_out"] = pack_tiles(np.concatenate([co, od_out[512:]], 0))
    d["od_mix"] = np.ascontiguousarray(a["od_d_mix_2"][0].transpose(1, 0, 2)).reshape(P, 512)
    d["consts"], where = stack_parts(constant_tables())
    d["even"], ewhere = stack_parts(even_tables())
    d["decay"] = decay_tables().astype(np.float32)
    d["window"] = window_tables().astype(np.float32)
    return d, where, ewhere


def kernel(**inputs):
    import concourse.bacc as _bacc
    from concourse import mybir as _mybir
    from concourse.bass_utils import run_bass_kernel_spmd as _run

    arrays, where, ewhere = layouts({k: np.asarray(v) for k, v in inputs.items()})
    nc = _bacc.Bacc("TRN2", target_bir_lowering=False, num_devices=1)
    feeds, ins = {}, {}
    for name, a in arrays.items():
        feeds[f"in_{name}"] = a
        ins[name] = nc.dram_tensor(f"in_{name}", a.shape, _mybir.dt.from_np(a.dtype), kind="ExternalInput").ap()
    out = nc.dram_tensor("out_t", (P, KC * SEQ), _mybir.dt.float32, kind="ExternalOutput").ap()
    program(nc, ins, out, where, ewhere)
    r = _run(nc, [feeds], core_ids=[0])
    got = r.results[0]["out_t"].reshape(P, KC, SEQ)
    return np.ascontiguousarray(got.transpose(2, 1, 0)).reshape(1, SEQ, D)
```

```python
import math
from contextlib import ExitStack

import numpy as np

import concourse.bass as bass
from concourse import mybir

F32 = mybir.dt.float32
FR = mybir.dt.float32r
I32 = mybir.dt.int32
ACT = mybir.ActivationFunctionType
ALU = mybir.AluOpType
AX = mybir.AxisListType

P = 128
D = 1024
KC = D // P
SEQ = 256
META = 16
TOK = META + SEQ
DEPTH = 2
CHUNK = 64
META_PAD = CHUNK - META
NEG = -1e30
GONE = -3e38

MOBA_H, DIFF_H, SB_H, X_H = 6, 4, 6, 4
MOBA_T, DIFF_T, SB_T = 3, 2, 3
D_FF = 2816
FT = D_FF // P
A_H, IDX_H, B_H, C_H = 8, 8, 8, 8
TOP_K = min(256, SEQ // 4)
EPS = 1e-6
EVEN_TILES = [("b", 0), ("a", 0), ("a", 1), ("b", 1), ("a", 2), ("b", 2), ("a", 3), ("b", 3)]
EVEN_ACTIVE = 6
SLAB = 1024

KB2 = [(0, 128), (128, 128), (256, 16)]


def rope_frequencies(theta, rot):
    return np.float32(1) / np.power(np.float32(theta), np.arange(0, rot, 2, dtype=np.float32) / np.float32(rot))


def signed_swap(head, half):
    m = np.zeros((P, P), np.float32)
    for b in range(0, P, head):
        for i in range(half):
            m[b + half + i, b + i] = -1.0
            m[b + i, b + half + i] = 1.0
    return m


def frequency_column(theta, head, rot):
    inv = rope_frequencies(theta, rot)
    col = np.zeros((P, 1), np.float32)
    for b in range(0, P, head):
        col[b:b + rot // 2, 0] = inv
        col[b + rot // 2:b + rot, 0] = inv
    return col


def constant_tables():
    i = np.arange(P)
    ident = np.eye(P, dtype=np.float32)
    ones = np.ones((P, P), np.float32)
    pair = (i[:, None] // 64 == i[None, :] // 64).astype(np.float32)
    later = (i[:, None] > i[None, :]).astype(np.float32)
    causal = np.concatenate([np.zeros((P, P)), np.where(i[None, :] <= i[:, None], 0.0, NEG)], 1)
    strict = (i[:, None] < i[None, :]).astype(np.float32)
    sb = np.concatenate([strict, ones, strict], 1)
    parts = [("ident", ident), ("ones", ones), ("pair", pair), ("later", later),
             ("swap64", signed_swap(64, 8)), ("swap32", signed_swap(32, 4)), ("swapr", signed_swap(64, 32)),
             ("causal", causal), ("sb", sb),
             ("inv64", frequency_column(500000.0, 64, 16)), ("inv32", frequency_column(500000.0, 32, 8)),
             ("eps", np.full((P, 1), EPS))]
    return parts


def even_tables():
    t = np.arange(TOK)
    cid = (t + META_PAD) // CHUNK
    adm = np.where(cid[None, :] <= cid[:, None], 0.0, NEG)
    adm = np.concatenate([adm, np.zeros((3 * P - TOK, TOK))], 0).reshape(3, P, TOK).transpose(1, 0, 2).reshape(P, 3 * TOK)
    inv = rope_frequencies(10000.0, 64)
    ang = t.astype(np.float32)[None, :] * inv[:, None]
    cos = np.cos(ang).astype(np.float32)[i4]
    sin = np.sin(ang).astype(np.float32)[i4]
    scale = np.float32(0.125)
    return [("adm", adm), ("cosq", cos), ("sinq", sin), ("cosk", cos * scale), ("sink", sin * scale)]


i4 = np.arange(P) % 32


def decay_tables():
    out = np.zeros((P, B_H, 432), np.float64)
    t = np.arange(TOK)
    for h in range(B_H):
        log_g = math.log(1.0 - 2.0 ** (-5.0 - h))
        at = 0
        for s0, n in KB2:
            rel = t[None, s0:] - t[s0:s0 + n, None]
            out[:n, h, at:at + TOK - s0] = np.where(rel >= 0, np.exp(np.maximum(rel, 0) * log_g), 0.0)
            at += TOK - s0
    return out.reshape(P, B_H * 432)


def window_tables():
    t = np.arange(TOK)
    cid = (t + META_PAD) // CHUNK
    q = cid[META:, None]
    ok = (t[None, :] < META) | ((cid[None, :] >= 1) & (cid[None, :] >= q - 2) & (cid[None, :] <= q))
    m = np.where(ok, 0.0, NEG).reshape(2, P, TOK).transpose(1, 0, 2)
    return m.reshape(P, 2 * TOK)


def stack_parts(parts):
    at, where = 0, {}
    for name, a in parts:
        where[name] = (at, a.shape[1])
        at += a.shape[1]
    return np.concatenate([a.astype(np.float32) for _, a in parts], 1), where


class Lane:

    def __init__(self, sem):
        self.sem, self.done, self.steps, self.reached = sem, 0, [], {}

    def needs(self, after):
        flat, stack = {}, list(after)
        while stack:
            m = stack.pop()
            if m is None:
                continue
            if isinstance(m, list):
                stack.extend(m)
                continue
            s, v = m
            if v > self.reached.get(s, 0):
                flat[s] = max(flat.get(s, 0), v)
        self.reached.update(flat)
        return list(flat.items())

    def step(self, issue, after=()):
        self.done += 1
        self.steps.append((self.needs(after), issue, self.sem, 1))
        return (self.sem, self.done)

    def load(self, issue, arrival, after=()):
        arrival.count += 16
        self.steps.append((self.needs(after), issue, arrival.sem, 16))
        return (arrival.sem, arrival.count)

    def play(self, eng):
        for waits, issue, sem, n in self.steps:
            for s, v in waits:
                eng.wait_ge(s, v)
            if sem is not None:
                issue(eng).then_inc(sem, n)
            elif issue is not None:
                issue(eng)


class Arrival:

    def __init__(self, sem):
        self.sem, self.count = sem, 0


class Ring:

    def __init__(self, bufs):
        self.bufs, self.free, self.at = bufs, [[] for _ in bufs], 0

    def take(self):
        i = self.at % len(self.bufs)
        self.at += 1
        marks, self.free[i] = self.free[i], None
        assert marks is not None, "the buffer's last reader is not queued yet"
        return i, self.bufs[i], marks

    def open(self, n=1):
        return all(self.free[(self.at + j) % len(self.bufs)] is not None for j in range(n))


class Split:

    def __init__(self, hi, lo, chunks):
        self.hi, self.lo = hi, lo
        self.ready = [None] * chunks
        self.free = []
        self.fresh = False

    def at(self, k, c0, n):
        return self.hi[:, k, c0:c0 + n], self.lo[:, k, c0:c0 + n]


class Joined:

    def __init__(self, a, b):
        self.a, self.b, self.cut = a, b, len(a.ready)

    @property
    def ready(self):
        return self.a.ready + self.b.ready

    @property
    def free(self):
        return self.a.free

    @free.setter
    def free(self, marks):
        self.a.free = self.b.free = marks

    @property
    def fresh(self):
        return self.a.fresh or self.b.fresh

    @fresh.setter
    def fresh(self, f):
        self.a.fresh = self.b.fresh = f

    def at(self, k, c0, n):
        return self.a.at(k, c0, n) if k < self.cut else self.b.at(k - self.cut, c0, n)


def program(nc, ins, out, where, ewhere):
    ctx = ExitStack()
    with ctx:
        def sem(name):
            return ctx.enter_context(nc.semaphore(name))

        def sb(name, shape, dt=F32, scope=ctx):
            return scope.enter_context(nc.sbuf_tensor(name, shape, dt))

        pe, act, dve, pool, sp = (Lane(sem(n)) for n in ("s_pe", "s_act", "s_dve", "s_pool", "s_sp"))

        h = sb("h", [P, KC, TOK])
        consts = sb("consts", [P, ins["consts"].shape[1]])
        cols = sb("cols", [P, ins["columns"].shape[1]])
        xa, xb = (Split(sb(f"x{i}_hi", [P, KC, TOK], FR), sb(f"x{i}_lo", [P, KC, TOK], FR), KC) for i in "ab")
        NRAW, NPART = 4, 4
        raw = [sb(f"w_raw{i}", [P, SLAB]) for i in range(NRAW)]
        w_hi = [sb(f"w_hi{i}", [P, SLAB], FR) for i in range(NPART)]
        w_lo = [sb(f"w_lo{i}", [P, SLAB], FR) for i in range(NPART)]
        squares = Ring([sb(f"square{i}", [P, TOK]) for i in range(3)])
        whole = Ring([sb(f"whole{i}", [P, TOK]) for i in range(3)])
        sumsq = Ring([sb(f"sumsq{i}", [P, TOK]) for i in range(3)])
        rstd = Ring([sb(f"rstd{i}", [P, TOK]) for i in range(3)])
        rstd_head = Ring([sb(f"rstd_head{i}", [P, TOK]) for i in range(2)])
        rstd_col = Ring([sb(f"rstd_col{i}", [P, 4]) for i in range(2)])
        probs = Ring([sb(f"prob{i}", [P, 2 * SEQ]) for i in range(5)])
        probs_t = Ring([sb(f"prob_t{i}", [P, 3 * P]) for i in range(3)])
        stats = Ring([sb(f"stat{i}", [P, 8]) for i in range(6)])

        bank = [ctx.enter_context(nc.psum_tensor(f"bank{i}", [P, 512], F32)) for i in range(8)]
        acc = Ring(bank[0:3])
        score = Ring(bank[3:5])
        turned = Ring(bank[5:6])
        mixed = Ring(bank[6:7])
        sums = Ring(bank[7:8])

        w_sem = [Arrival(sem(f"s_w{i}")) for i in range(NRAW)]
        setup = Arrival(sem("s_setup"))
        setup_ready = [(setup.sem, 16)]
        tables = Arrival(sem("s_tables"))
        out_sem = Arrival(sem("s_out"))

        def const(name, c0=0, n=None):
            at, width = where[name]
            return consts[:, at + c0:at + (width if n is None else c0 + n)]

        def col(name, c=0, p0=0, pn=P):
            at = COLUMNS[name]
            return cols[p0:p0 + pn, at + c:at + c + 1]

        def activate(o, i, func, after, scale=1.0, bias=0.0, total=None):
            if total is None:
                return act.step(lambda e: e.activation(o, i, func, scale=scale, bias=bias), after)
            return act.step(lambda e: e.activation(o, i, func, scale=scale, bias=bias, accum_out=total), after)

        def copy_act(o, i, after):
            return act.step(lambda e: e.activation(o, i, ACT.Copy), after)

        def copy_dve(o, i, after):
            return dve.step(lambda e: e.tensor_copy(o, i), after)

        def pairwise(o, a, b, op, after, lane=dve):
            return lane.step(lambda e: e.tensor_tensor(o, a, b, op), after)

        def scaled(o, a, s1, op0, after, s2=None, op1=None):
            if op1 is None:
                return dve.step(lambda e: e.tensor_scalar(o, a, s1, None, op0), after)
            return dve.step(lambda e: e.tensor_scalar(o, a, s1, s2, op0, op1), after)

        def fused(o, a, s, b, op0, op1, after):
            return dve.step(lambda e: e.scalar_tensor_tensor(out=o, in0=a, scalar=s, in1=b, op0=op0, op1=op1), after)

        def reciprocal(o, a, after):
            return dve.step(lambda e: e.reciprocal(o, a), after)

        def product(o, pairs, after):
            def issue(e):
                for n, (lhsT, rhs) in enumerate(pairs):
                    mm = e.matmul(o, lhsT, rhs, start=(n == 0), stop=(n == len(pairs) - 1))
                return mm
            return pe.step(issue, after)

        cols_ready = [sp.load(lambda e: e.dma_start(cols[:, :], ins["columns"]), Arrival(sem("s_cols")))]

        plan = []

        def tiles_plan(src, tiles, k):
            for t in tiles:
                for k0 in range(0, k // P, 8):
                    kn = min(8, k // P - k0)
                    plan.append((src[t][:, k0 * P:(k0 + kn) * P], kn * P))

        def rows_plan(src, n):
            per = SLAB // n
            for k0 in range(0, KC, per):
                kn = min(per, KC - k0)
                plan.append((src[:, k0 * n:(k0 + kn) * n], kn * n))

        def memory_plan(l):
            tiles_plan(ins["w_xk"][l], range(4), D)
            rows_plan(ins["w_xv"][l], 512)

        memory_plan(0)
        for l in range(DEPTH):
            tiles_plan(ins["w_in"][l], [0, 3], D)
            rows_plan(ins["w_moba_v"][l], MOBA_H * 64)
            tiles_plan(ins["w_in"][l], [1, 4, 2, 5, 12, 14], D)
            rows_plan(ins["w_diff_v"][l], DIFF_H * 64)
            tiles_plan(ins["w_in"][l], [13, 15, 20, 23], D)
            rows_plan(ins["w_sb_v"][l], SB_H * 64)
            tiles_plan(ins["w_in"][l], [21, 24, 22, 25, 9, 10, 11, 18, 19, 29, 30, 31], D)
            tiles_plan(ins["w_out"][l], range(8), D)
            tiles_plan(ins["w_xq"][l], range(4), D)
            if l == 0:
                memory_plan(1)
            tiles_plan(ins["w_xo"][l], range(8), 512)

        def ffn_plan(name, l):
            tiles_plan(ins[name + "_in"][l], range(2 * FT), D)
            tiles_plan(ins[name + "_out"][l], range(8), D_FF)

        ffn_plan("ffn1", 0)
        tiles_plan(ins["ev_in"], range(0, 5), D)
        plan.append((ins["ev_iw"], KC * IDX_H))
        for kind, t in EVEN_TILES:
            tiles_plan(ins["ev_in"], [5 + t, 9 + t, 13 + t] if kind == "a" else
                       [17 + t, 21 + t, 25 + 2 * t, 33 + 2 * t, 26 + 2 * t, 34 + 2 * t], D)
        tiles_plan(ins["ev_out"], range(8), 1536)
        ffn_plan("ffn2", 0)
        ffn_plan("ffn1", 1)
        tiles_plan(ins["od_in"], [4, 5, 0, 1, 2, 3, 6, 7, 8, 9], D)
        tiles_plan(ins["od_out"], range(8), D)
        ffn_plan("ffn2", 1)

        converted = [None] * len(plan)
        raw_free = [[] for _ in range(NRAW)]
        part_free = [[] for _ in range(NPART)]
        landed = [None] * len(plan)
        state = {"use": 0, "fetch": 0, "convert": 0}

        def fetch():
            i = state["fetch"]
            if i >= len(plan):
                return
            src, width = plan[i]
            landed[i] = sp.load(lambda e: e.dma_start(raw[i % NRAW][:, 0:width], src), w_sem[i % NRAW], raw_free[i % NRAW])
            state["fetch"] += 1

        def convert():
            settle()
            i = state["convert"]
            if i >= len(plan):
                return
            width = plan[i][1]
            w, hi, lo = raw[i % NRAW][:, 0:width], w_hi[i % NPART][:, 0:width], w_lo[i % NPART][:, 0:width]
            top = copy_act(hi, w, [landed[i], part_free[i % NPART]])
            unsettled.append((i, w, hi, lo, top))
            state["convert"] += 1

        def settle():
            while unsettled:
                i, w, hi, lo, top = unsettled.pop()
                rest = pairwise(lo, w, hi.bitcast(F32), ALU.subtract, [top])
                converted[i] = [top, rest]
                raw_free[i % NRAW] = [top, rest]
                fetch()

        unsettled = []
        def slab(width):
            i = state["use"]
            assert plan[i][1] == width, (i, plan[i][1], width)
            state["use"] += 1
            return i, w_hi[i % NPART], w_lo[i % NPART], converted[i]

        def slab_done(i, mark):
            part_free[i % NPART] = [mark]
            if i > 0:
                convert()

        def three_products(e, o, w_h, w_l, a_h, a_l, first, last):
            e.matmul(o, w_h, a_h, start=first, stop=False)
            e.matmul(o, w_h, a_l, start=False, stop=False)
            return e.matmul(o, w_l, a_h, start=False, stop=last)

        def weight_tile(src, k, c0, n):
            b, o, free = acc.take()
            for k0 in range(0, k, 8):
                kn = min(8, k - k0)
                i, wh, wl, there = slab(kn * P)
                group = 1 if src.fresh else kn
                for g0 in range(0, kn, group):
                    def issue(e, k0=k0, g0=g0, group=group, wh=wh, wl=wl):
                        for j in range(g0, g0 + group):
                            w = slice(j * P, (j + 1) * P)
                            mm = three_products(e, o[:, 0:n], wh[:, w], wl[:, w], *src.at(k0 + j, c0, n),
                                                k0 + j == 0, k0 + j == k - 1)
                        return mm
                    mark = pe.step(issue, [there, free, src.ready[k0 + g0:k0 + g0 + group]])
                slab_done(i, mark)
            src.free, src.fresh = [mark], False
            return b, o, mark

        def weight_rows(src, n, blocks, c0=0):
            per = min(KC, SLAB // n)
            banks = [acc.take() for _ in blocks]
            for k0 in range(0, KC, per):
                kn = min(per, KC - k0)
                i, wh, wl, there = slab(kn * n)

                def issue(e, k0=k0, kn=kn, wh=wh, wl=wl):
                    for (t0, tn), (_, o, _) in zip(blocks, banks):
                        for j in range(kn):
                            w = slice(j * n, (j + 1) * n)
                            t = slice(c0 + t0, c0 + t0 + tn)
                            k = k0 + j
                            a_hi, a_lo = src.at(k, t.start, tn)
                            e.matmul(o[0:tn, 0:n], a_hi, wh[:, w], start=(k == 0), stop=False)
                            e.matmul(o[0:tn, 0:n], a_lo, wh[:, w], start=False, stop=False)
                            mm = e.matmul(o[0:tn, 0:n], a_hi, wl[:, w], start=False, stop=(k == KC - 1))
                    return mm
                mark = pe.step(issue, [there, [f for _, _, f in banks], src.ready[k0:k0 + kn]])
                slab_done(i, mark)
            src.free = [mark]
            return [(b, o) for b, o, _ in banks], mark

        later = []

        def flush():
            todo = list(later)
            later.clear()
            for f in todo:
                f()

        def split(y, y_mark, dst, k, c0, n, slot, urgent=False):
            hi, lo = dst.hi[:, k, c0:c0 + n], dst.lo[:, k, c0:c0 + n]
            top = copy_act(hi, y, [y_mark, dst.free])
            rest = pairwise(lo, y, hi.bitcast(F32), ALU.subtract, [top], lane=dve if urgent else pool)
            if slot is not None:
                whole.free[slot] = [top, rest]
            dst.ready[k], dst.fresh = [top, rest], True

        class Norm:

            def __init__(self, c0, n, chunks=KC, lhs="ones"):
                self.c0, self.n, self.chunks, self.seen, self.lhs = c0, n, chunks, 0, lhs
                self.ring = rstd if chunks > 1 else rstd_head

            def square(self, src, ready):
                k, n = self.seen, self.n
                self.seen += 1
                if k == 0:
                    self.q, self.total, free = sumsq.take()
                    self.added = activate(self.total[:, 0:n], src, ACT.Square, [ready, free])
                    return
                s, sq, free = squares.take()
                m = activate(sq[:, 0:n], src, ACT.Square, [ready, free])
                self.added = pairwise(self.total[:, 0:n], self.total[:, 0:n], sq[:, 0:n], ALU.add, [m, self.added],
                                      lane=pool)
                squares.free[s] = [self.added]

            def finish(self, width):
                n = self.n
                b, o, free = sums.take()
                mm = product(o[:, 0:n], [(const(self.lhs), self.total[:, 0:n])], [self.added, free, setup_ready])
                sumsq.free[self.q] = [mm]
                self.r, self.rs, rfree = self.ring.take()
                ln = activate(self.rs[:, 0:n], o[:, 0:n], ACT.Ln, [mm, rfree], scale=1.0 / width, bias=const("eps"))
                sums.free[b] = [ln]
                self.mark = activate(self.rs[:, 0:n], self.rs[:, 0:n], ACT.Exp, [ln], scale=-0.5)

            def column(self, blocks):
                b, o, free = sums.take()
                i, self.col, cfree = rstd_col.take()
                for j, (t0, tn) in enumerate(blocks):
                    mm = product(o[0:tn, j:j + 1], [(self.rs[0:1, t0:t0 + tn], const("ones")[0:1, 0:1])],
                                 [self.mark, free, setup_ready])
                ms = [copy_dve(self.col[0:tn, j:j + 1], o[0:tn, j:j + 1], [mm, cfree]) for j, (_, tn) in enumerate(blocks)]
                sums.free[b] = ms
                self.col_ready, self.col_slot = ms, i

            def scale(self, dst, o, after):
                self.last = pairwise(dst, o, self.rs[:, 0:self.n], ALU.mult, [self.mark, after])
                self.ring.free[self.r] = [self.last]
                return self.last

        def feed(k, gain, dst, c0, n, ready, src=None, urgent=False):
            s, y, free = whole.take()
            ym = scaled(y[:, 0:n], h[:, k, c0:c0 + n] if src is None else src, col(gain, k), ALU.mult,
                        [ready, free, cols_ready])
            split(y[:, 0:n], ym, dst, k, c0, n, s, urgent)

        def add_to_h(src, k, c0, n, factor=1.0, norm=None, feeds=None, column=None):
            for m in range(KC):
                b, o, mark = weight_tile(src, k, c0, n)
                flush()
                h_ready[m] = fused(h[:, m, c0:c0 + n], o[:, 0:n], factor, h[:, m, c0:c0 + n], ALU.mult, ALU.add,
                                   [mark, h_ready[m]])
                acc.free[b] = [h_ready[m]]
                if feeds is not None:
                    feed(m, feeds[0], feeds[1], norm.c0, norm.n, h_ready[m], urgent=(m == KC - 1))
                settle()
                if norm is not None:
                    norm.square(h[:, m, norm.c0:norm.c0 + norm.n], h_ready[m])
            if feeds is not None:
                later.append(lambda: norm.finish(D))
                if column:
                    later.append(lambda: norm.column(column))

        def weave(units, filler, active=3, every=1):
            waiting, running = list(units), []
            filling, rounds = True, 0
            while waiting or running:
                while waiting and len(running) < active:
                    running.append(waiting.pop(0))
                    break
                running = [u for u in running if next(u, None) is not None]
                rounds += 1
                if filling and rounds % every == 0 and next(filler, None) is None:
                    filling = False
                    flush()
            while filling and next(filler, None) is not None:
                pass
            flush()

        def chain(*gens):
            for g in gens:
                for v in g:
                    yield v

        def when(there, gen):
            while not there():
                yield True
            for v in (gen() if callable(gen) else gen):
                yield v

        def turn_and_mix(p, p_mark, nq, kblocks, values, v_marks, place, write):
            while not (turned.open() and probs_t.open()):
                yield None
            t, tb, free = turned.take()

            def issue(e):
                for j, (k0, kn) in enumerate(kblocks):
                    mm = e.transpose(tb[0:kn, j * P:j * P + nq], p[0:nq, k0:k0 + kn], const("ident")[0:nq, 0:nq])
                return mm
            tm = pe.step(issue, [p_mark, free, setup_ready])
            s, pt, sfree = probs_t.take()
            full = len([1 for _, kn in kblocks if kn == P])
            marks = []
            if nq == P:
                marks.append(copy_act(pt[:, 0:full * P], tb[:, 0:full * P], [tm, sfree]))
            else:
                v3 = lambda a: a[:, 0:full * P].rearrange("p (j q) -> p j q", q=P)[:, :, 0:nq]
                marks.append(copy_act(v3(pt), v3(tb), [tm, sfree]))
            if full < len(kblocks):
                kn = kblocks[-1][1]
                marks.append(copy_act(pt[0:kn, full * P:full * P + nq], tb[0:kn, full * P:full * P + nq], [tm, sfree]))
            turned.free[t] = marks
            yield tm
            b, o, ofree = mixed.take()
            p0, pn = place
            pairs = [(values[j], pt[0:kn, j * P:j * P + nq]) for j, (_, kn) in enumerate(kblocks)]
            mm = product(o[p0:p0 + pn, 0:nq], pairs, [marks, ofree, v_marks])
            probs_t.free[s] = [mm]
            mixed.free[b] = [write(o[p0:p0 + pn, 0:nq], mm)]

        def attend(q, k, qk_marks, nq, nk, kblocks, bias, bias_marks, scale, values, v_marks, place, write, sink=None):
            while not (probs.open() and score.open() and stats.open()):
                yield True
            b, o, free = score.take()
            sm = product(o[0:nq, 0:nk], [(q, k)], [qk_marks, free])
            pi, p, pfree = probs.take()
            si, st, sfree = stats.take()
            mx, shift, total, inv = (st[0:nq, c:c + 1] for c in (0, 1, 2, 3))
            if bias is None:
                m1 = dve.step(lambda e: e.tensor_reduce(mx, o[0:nq, 0:nk], AX.X, ALU.max), [sm, sfree])
                src, read = o[0:nq, 0:nk], [sm]
            else:
                m1 = dve.step(lambda e: e.tensor_tensor_reduce(p[0:nq, 0:nk], o[0:nq, 0:nk], bias, 1.0, GONE, ALU.add,
                                                               ALU.max, mx), [sm, pfree, sfree, bias_marks])
                src, read = p[0:nq, 0:nk], [m1]
            if sink is None:
                m2 = scaled(shift, mx, -scale, ALU.mult, [m1])
            else:
                m2 = scaled(mx, mx, scale, ALU.mult, [m1], sink, ALU.max)
                m2 = scaled(shift, mx, -1.0, ALU.mult, [m2])
            ex = activate(p[0:nq, 0:nk], src, ACT.Exp, [m2, read, pfree], scale=scale, bias=shift, total=total)
            score.free[b] = [ex if bias is None else m1]
            if sink is not None:
                es = activate(st[0:nq, 4:5], sink, ACT.Exp, [m2], bias=shift)
                ex = pairwise(total, total, st[0:nq, 4:5], ALU.add, [ex, es])
            m3 = reciprocal(inv, total, [ex])
            pm = scaled(p[0:nq, 0:nk], p[0:nq, 0:nk], inv, ALU.mult, [m3, ex])
            stats.free[si] = [pm]
            yield pm
            yield True
            turn = turn_and_mix(p, pm, nq, kblocks, values, v_marks, place, write)
            for m in turn:
                probs.free[pi] = [m] if m else None
                yield True

        scratch = {}

        def turned_tile(norm, dst, ready, table, swap, c0, n, before=()):
            def gen(src):
                b, o, mark = weight_tile(src, KC, c0, n)
                flush()
                r, rq, free = scratch["raw"].take()
                m = norm.scale(rq[:, 0:n], o[:, 0:n], [mark, free])
                acc.free[b] = [m]

                def rotate():
                    b2, o2, free2 = acc.take()
                    mm = product(o2[:, 0:n], [(const(swap), rq[:, 0:n])], [m, free2, setup_ready])
                    t_, tq, tfree = scratch["turn"].take()
                    a = pairwise(dst, rq[:, 0:n], table[0], ALU.mult, [m, table[2], list(before)], lane=pool)
                    c = pairwise(tq[:, 0:n], o2[:, 0:n], table[1], ALU.mult, [mm, tfree, table[2]])
                    acc.free[b2] = [c]
                    d = pairwise(dst, dst, tq[:, 0:n], ALU.add, [a, c], lane=pool)
                    scratch["raw"].free[r] = [mm, a]
                    scratch["turn"].free[t_] = [d]
                    ready.append(d)
                later.append(rotate)
            return gen

        def silu_tile(norm, dst, ready, c0, n, before=()):
            def gen(src):
                b, o, mark = weight_tile(src, KC, c0, n)
                flush()
                r, g, free = scratch["raw"].take()
                gm = norm.scale(g[:, 0:n], o[:, 0:n], [mark, free])
                acc.free[b] = [gm]
                m = activate(dst, g[:, 0:n], ACT.Exp, [gm, list(before)], scale=-1.0)
                m = scaled(dst, dst, 1.0, ALU.add, [m])
                m = reciprocal(dst, dst, [m])
                m = pairwise(dst, dst, g[:, 0:n], ALU.mult, [m], lane=pool)
                scratch["raw"].free[r] = [m]
                ready.append(m)
            return gen

        def plain_tile(norm, dst, ready, c0, n):
            def gen(src):
                b, o, mark = weight_tile(src, KC, c0, n)
                flush()
                m = norm.scale(dst, o[:, 0:n], [mark])
                acc.free[b] = [m]
                ready.append(m)
            return gen

        def rows_step(norm, dst, ready, n, c0, blocks):
            def gen(src):
                banks, mark = weight_rows(src, n, blocks, c0)
                flush()
                for tb, (b, o) in enumerate(banks):
                    m = activate(dst[:, tb, :], o[:, 0:n], ACT.Copy, [mark, norm.col_ready], scale=norm.col[:, tb:tb + 1])
                    acc.free[b] = [m]
                    ready.append(m)
                rstd_col.free[norm.col_slot] = [m]
            return gen

        def run_on(tiles, src):
            for t in tiles:
                t(src)
                settle()
                yield True

        def run(tiles, src):
            for _ in run_on(tiles, src):
                yield True
            flush()

        def normed_tile(norm, dst, ready, gain, c0, n):
            def gen(src):
                b, o, mark = weight_tile(src, KC, c0, n)
                flush()
                m = norm.scale(dst, o[:, 0:n], [mark])
                acc.free[b] = [m]
                nm = Norm(0, n, 1, "pair")
                nm.square(dst, m)

                def scale():
                    nm.finish(64)
                    w = fused(dst, dst, col(gain), nm.rs[:, 0:n], ALU.mult, ALU.mult, [nm.mark])
                    nm.ring.free[nm.r] = [w]
                    ready.append(w)
                later.append(scale)
            return gen

        def value_tile(norm, dst, ready, f0, before=()):
            def gen(src):
                b, o, mark = weight_tile(src, KC, 0, TOK)
                flush()
                r, rv, free = scratch["raw"].take()
                m = norm.scale(rv[:, 0:TOK], o[:, 0:TOK], [mark, free])
                acc.free[b] = [m]

                def turn():
                    t, tb, tfree = turned.take()

                    def issue(e):
                        for j, (k0, kn) in enumerate(KB2):
                            mm = e.transpose(tb[0:kn, j * P:(j + 1) * P], rv[:, k0:k0 + kn], const("ident"))
                        return mm
                    tm = pe.step(issue, [m, tfree, setup_ready])
                    scratch["raw"].free[r] = [tm]
                    w1 = copy_act(dst[:, 0:2, f0:f0 + P], tb[:, 0:2 * P].rearrange("p (j f) -> p j f", j=2), [tm, list(before)])
                    w2 = copy_act(dst[0:16, 2, f0:f0 + P], tb[0:16, 2 * P:3 * P], [tm, list(before)])
                    turned.free[t] = [w1, w2]
                    ready.extend([w1, w2])
                later.append(turn)
            return gen

        C0, N = META, SEQ
        QB = [(0, P), (P, P)]
        with ExitStack() as s1:
            sb1 = lambda name, shape, dt=F32: sb(name, shape, dt, s1)
            rope = {n: sb1("rope_" + n, [P, SEQ]) for n in ("cos64", "sin64", "cos32", "sin32")}
            scratch["raw"] = Ring([sb1(f"raw_qk{i}", [P, SEQ]) for i in range(3)])
            scratch["turn"] = Ring([sb1(f"turn_qk{i}", [P, SEQ]) for i in range(2)])
            mq, mk = sb1("moba_q", [P, MOBA_T, SEQ]), sb1("moba_k", [P, MOBA_T, SEQ])
            dq, dk = sb1("diff_q", [P, DIFF_T, SEQ]), sb1("diff_k", [P, DIFF_T, SEQ])
            sq_, sk = sb1("sb_q", [P, SB_T, SEQ]), sb1("sb_k", [P, SB_T, SEQ])
            mv, dv, sv = sb1("moba_v", [P, 2, 384]), sb1("diff_v", [P, 2, 256]), sb1("sb_v", [P, 2, 384])
            xk = [sb1(f"cross_k{l}", [P, X_H, SEQ]) for l in range(DEPTH)]
            xv = [sb1(f"cross_v{l}", [P, 2, 512]) for l in range(DEPTH)]
            gate = sb1("gate", [P, 8, SEQ])
            mix = sb1("mix", [P, 8, SEQ])
            stick = Ring([sb1(f"stick{i}", [P, 3, 384]) for i in range(3)])
            lam_t = sb1("lam_t", [P, 8])
            lam_p = sb1("lam_p", [P, 2, 32])
            pos_i, pos, angle, turns = mix[:, 0, :].bitcast(I32), mix[:, 1, :], mix[:, 2, :], mix[:, 3, :]

            mem_t = gate

            def load_halves(dst, name, c0, n, after=()):
                src, marks = ins[name].rearrange("p (c t) -> p c t", c=KC), []
                for i in range(2):
                    k = slice(i * KC // 2, (i + 1) * KC // 2)
                    m = sp.load(lambda e, k=k: e.dma_start(dst[:, k, c0:c0 + n], src[:, k, :]),
                                Arrival(sem(f"s_{name}_{sp.done}_{len(sp.steps)}")), after)
                    marks += (KC // 2) * [m]
                return marks

            act.steps.append(([], lambda e: e.preload_act_table_set("natural_log_exp_and_others"), None, 0))
            mem_loaded = load_halves(mem_t, "mem_t", 0, SEQ)
            fetch()
            fetch()
            sp.load(lambda e: e.dma_start(consts[:, :], ins["consts"]), setup)
            for _ in range(NRAW - 2):
                fetch()
            x_loaded = load_halves(h, "x_t", META, SEQ)
            meta_loaded = sp.load(lambda e: e.dma_start(h[:, :, 0:META], ins["meta_t"].rearrange("p (c t) -> p c t", c=KC)),
                                  Arrival(sem("s_meta")))
            h_ready = list(x_loaded)
            pos_loaded = sp.load(lambda e: e.dma_start(pos_i, ins["positions"].to_broadcast([P, SEQ])),
                                 Arrival(sem("s_pos")))

            def feed_memory(l, dst, loaded, slabs=0):
                nm = Norm(0, SEQ)
                for k in range(KC):
                    feed(k, f"memg{l}", dst, 0, SEQ, loaded[k], src=mem_t[:, k, :], urgent=(k % 2 == 0))
                    if k % 4 == 3 and slabs:
                        convert()
                        settle()
                        slabs -= 1
                for k in range(KC):
                    nm.square(mem_t[:, k, :], [loaded[k]])
                later.append(lambda: nm.finish(D))
                later.append(lambda: nm.column(QB))
                return nm

            def memory_tiles(l, nm, r_xk, r_xv):
                return ([plain_tile(nm, xk[l][:, t, :], r_xk, 0, SEQ) for t in range(X_H)]
                        + [rows_step(nm, xv[l], r_xv, 512, 0, QB)])

            r_xk, r_xv = [[], []], [[], []]
            nm = feed_memory(0, xb, mem_loaded, 2)
            for _ in range(NPART - 2):
                convert()
                settle()
            memory = run(memory_tiles(0, nm, r_xk[0], r_xv[0]), xb)
            next(memory)
            norm = Norm(C0, N)
            for k in range(KC):
                feed(k, "attn0", xa, C0, N, x_loaded[k])
            next(memory)
            for k in range(KC):
                norm.square(h[:, k, C0:TOK], [x_loaded[k]])
            later.append(lambda: norm.finish(D))
            later.append(lambda: norm.column(QB))
            next(memory)
            pm = copy_dve(pos, pos_i, [pos_loaded])
            C1 = 6.28125
            C2 = float(np.float32(np.float64(int((2 * math.pi - C1) * 2 ** 21)) / 2 ** 21))
            C3 = float(np.float32(2 * math.pi - C1 - C2))
            MAGIC = 1.5 * 2 ** 23
            last = [pm, setup_ready]
            for inv, suffix in (("inv64", "64"), ("inv32", "32")):
                for name, quarter in (("cos", 0.25), ("sin", 0.0)):
                    a = scaled(angle, pos, const(inv), ALU.mult, [last])
                    t = scaled(turns, angle, 1.0 / (2 * math.pi), ALU.mult, [a], quarter, ALU.add)
                    t = scaled(turns, turns, MAGIC, ALU.add, [t])
                    t = scaled(turns, turns, -MAGIC, ALU.add, [t])
                    for c in (C1, C2, C3):
                        t = fused(angle, turns, -c, angle, ALU.mult, ALU.add, [t])
                    if quarter:
                        t = scaled(angle, angle, math.pi / 2, ALU.add, [t])
                    t = scaled(angle, angle, -3.1415925, ALU.max, [t], 3.1415925, ALU.min)
                    rope_mark = activate(rope[name + suffix][:, :], angle, ACT.Sin, [t])
                    last = [rope_mark]
                    next(memory, None)
            for _ in memory:
                pass
            lam = []
            for l in range(DEPTH):
                lam_init = 0.8 - 0.6 * math.exp(-0.3 * l)
                at = COLUMNS["lambda"] + l * 128
                m = None
                for j in range(2):
                    q1, k1 = cols[:, at + 64 * j:at + 64 * j + 32], cols[:, at + 64 * j + 32:at + 64 * j + 64]
                    m = pairwise(lam_p[:, j, :], q1, k1, ALU.mult, [setup_ready, m, lam])
                m = dve.step(lambda e, l=l: e.tensor_reduce(lam_t[:, 4 * l:4 * l + 2], lam_p[:, :, :], AX.X, ALU.add), [m])
                m = activate(lam_t[:, 4 * l:4 * l + 2], lam_t[:, 4 * l:4 * l + 2], ACT.Exp, [m])
                m = pairwise(lam_t[:, 4 * l + 2:4 * l + 3], lam_t[:, 4 * l + 1:4 * l + 2], lam_t[:, 4 * l:4 * l + 1],
                             ALU.subtract, [m])
                m = scaled(lam_t[:, 4 * l + 2:4 * l + 3], lam_t[:, 4 * l + 2:4 * l + 3], -lam_init, ALU.add, [m])
                lam = [scaled(lam_t[:, 4 * l + 3:4 * l + 4], col("head_gain", l), 1.0 - lam_init, ALU.mult, [m])]
            lam_ready = lam

            act.steps.append(([], lambda e: e.preload_act_table_set("natural_log_exp_and_others"), None, 0))
            cs64 = (rope["cos64"][:, :], rope["sin64"][:, :], [rope_mark])
            cs32 = (rope["cos32"][:, :], rope["sin32"][:, :], [rope_mark])
            x, other = xa, xb
            for l in range(DEPTH):
                r_mqk, r_mv, r_dqk, r_dv, r_sqk, r_sv, r_gate = ([] for _ in range(7))
                mixed_marks = [[] for _ in range(8)]

                def moba_unit(hd, qb, r_mqk=r_mqk, r_mv=r_mv, mixed_marks=mixed_marks):
                    t, p0 = hd // 2, (hd % 2) * 64
                    nk = P * (qb + 1)

                    def write(o, m):
                        w = copy_act(mix[p0:p0 + 64, t, qb * P:(qb + 1) * P], o, [m])
                        mixed_marks[t].append(w)
                        return w
                    return attend(mq[p0:p0 + 64, t, qb * P:(qb + 1) * P], mk[p0:p0 + 64, t, 0:nk], r_mqk, P, nk,
                                  QB[:qb + 1], const("causal", P * (1 - qb), nk), setup_ready, 64 ** -0.5,
                                  [mv[:, j, hd * 64:(hd + 1) * 64] for j in range(qb + 1)], r_mv, (p0, 64), write)

                def diff_unit(hd, qb, l=l):
                    nk = P * (qb + 1)
                    scale = 32 ** -0.5
                    t = hd // 2
                    while not (probs.open() and score.open() and stats.open()):
                        yield True
                    b, o, free = score.take()
                    pi, p, pfree = probs.take()
                    si, st, sfree = stats.take()
                    sc = []
                    for c in range(2):
                        p0 = ((2 * hd + c) % 4) * 32
                        sc.append(product(o[:, c * nk:(c + 1) * nk],
                                          [(dq[p0:p0 + 32, t, qb * P:(qb + 1) * P], dk[p0:p0 + 32, t, 0:nk])],
                                          [r_dqk, free, list(sc)]))
                    ms = []
                    for c in range(2):
                        ms.append(dve.step(lambda e, c=c: e.tensor_tensor_reduce(
                            p[:, c * nk:(c + 1) * nk], o[:, c * nk:(c + 1) * nk], const("causal", P * (1 - qb), nk), 1.0,
                            GONE, ALU.add, ALU.max, st[:, c:c + 1]), [sc[1], pfree, sfree, setup_ready]))
                    score.free[b] = [ms[1]]
                    m2 = scaled(st[:, 2:4], st[:, 0:2], -scale, ALU.mult, ms)
                    ex = [activate(p[:, c * nk:(c + 1) * nk], p[:, c * nk:(c + 1) * nk], ACT.Exp, [m2], scale=scale,
                                   bias=st[:, 2 + c:3 + c], total=st[:, 4 + c:5 + c]) for c in range(2)]
                    m3 = reciprocal(st[:, 6:8], st[:, 4:6], ex)
                    m4 = scaled(st[:, 7:8], st[:, 7:8], lam_t[:, 4 * l + 2:4 * l + 3], ALU.mult, [m3, lam_ready])
                    m5 = scaled(p[:, 0:nk], p[:, 0:nk], st[:, 6:7], ALU.mult, [m3])
                    pm_ = fused(p[:, 0:nk], p[:, nk:2 * nk], st[:, 7:8], p[:, 0:nk], ALU.mult, ALU.add, [m4, m5])
                    stats.free[si] = [pm_]
                    yield pm_
                    yield True

                    def write(o_, m):
                        w = copy_act(mix[(hd % 2) * 64:(hd % 2) * 64 + 64, MOBA_T + t, qb * P:(qb + 1) * P], o_, [m])
                        mixed_marks[MOBA_T + t].append(w)
                        return w
                    turn = turn_and_mix(p, pm_, P, QB[:qb + 1], [dv[:, j, hd * 64:(hd + 1) * 64] for j in range(qb + 1)],
                                        r_dv, ((hd % 2) * 64, 64), write)
                    for m in turn:
                        probs.free[pi] = [m] if m else None
                        yield True

                def diff_norm(t, l=l):
                    tile = mix[:, MOBA_T + t, :]
                    nm = Norm(0, SEQ, 1, "pair")
                    nm.square(tile, mixed_marks[MOBA_T + t])
                    yield True
                    nm.finish(64)
                    w = fused(tile, tile, lam_t[:, 4 * l + 3:4 * l + 4], nm.rs[:, 0:SEQ], ALU.mult, ALU.mult,
                              [nm.mark, lam_ready])
                    nm.ring.free[nm.r] = [w]
                    mixed_marks[MOBA_T + t].append(w)

                def stick_unit(hd):
                    t, p0 = hd // 2, (hd % 2) * 64
                    scale = 64 ** -0.5
                    q, k = sq_[p0:p0 + 64, t, :], sk[p0:p0 + 64, t, :]
                    while not (stick.open() and score.open()):
                        yield True
                    si, st, sfree = stick.take()
                    b, o, free = score.take()
                    z0 = product(o[:, 0:256], [(k[:, 0:P], q)], [r_sqk, free])
                    z1 = product(o[:, 256:384], [(k[:, P:], q[:, P:])], [z0])
                    z = o[:, 0:384]
                    soft, log_beta, log_rest = st[:, 0, :], st[:, 1, :], st[:, 2, :]
                    mag = activate(soft, z, ACT.Abs, [z1, sfree], scale=scale)
                    m = activate(soft, soft, ACT.Exp, [mag], scale=-1.0)
                    m = activate(soft, soft, ACT.Ln, [m], bias=1.0)
                    lb = scaled(log_beta, z, scale, ALU.mult, [mag, sfree], 0.0, ALU.min)
                    lb = pairwise(log_beta, log_beta, soft, ALU.subtract, [m, lb])
                    lr = fused(log_rest, z, -scale, log_beta, ALU.mult, ALU.add, [lb])
                    score.free[b] = [lr]
                    lr = pairwise(log_rest, log_rest, const("sb"), ALU.mult, [lr, setup_ready])
                    yield True
                    yield True
                    b2, o2, free2 = score.take()

                    def between(e):
                        e.matmul(o2[:, 0:256], const("later"), log_rest[:, 0:256], start=True, stop=False)
                        e.matmul(o2[:, P:256], const("ones"), log_rest[:, 256:384], start=False, stop=True)
                        return e.matmul(o2[:, 256:384], const("later"), log_rest[:, 256:384], start=True, stop=True)
                    bm = pe.step(between, [lr, free2, setup_ready])
                    w = pairwise(soft, o2[:, 0:384], log_beta, ALU.add, [bm, lb, m])
                    score.free[b2] = [w]
                    w = activate(soft, soft, ACT.Exp, [w])
                    w = pairwise(soft, soft, const("sb"), ALU.mult, [w, setup_ready])
                    yield True
                    yield True
                    b3, o3, free3 = mixed.take()

                    def values(e):
                        e.matmul(o3[p0:p0 + 64, 0:256], sv[:, 0, hd * 64:(hd + 1) * 64], soft[:, 0:256], start=True, stop=False)
                        return e.matmul(o3[p0:p0 + 64, P:256], sv[:, 1, hd * 64:(hd + 1) * 64], soft[:, 256:384],
                                        start=False, stop=True)
                    vm = pe.step(values, [w, free3, r_sv])
                    stick.free[si] = [vm]
                    wr = copy_act(mix[p0:p0 + 64, MOBA_T + DIFF_T + t, :], o3[p0:p0 + 64, 0:256], [vm])
                    mixed.free[b3] = [wr]
                    mixed_marks[MOBA_T + DIFF_T + t].append(wr)

                def merge(t):
                    s, y, free = whole.take()
                    ym = pairwise(y[:, 0:N], mix[:, t, :], gate[:, t, :], ALU.mult, [mixed_marks[t], r_gate, free])
                    split(y[:, 0:N], ym, other, t, C0, N, s)
                    merged.append(ym)
                    yield True

                merged = []
                d0, s0 = MOBA_T, MOBA_T + DIFF_T
                turn_to = lambda d, t, r, cs, sw: turned_tile(norm, d[:, t, :], r, cs, sw, C0, N)
                moba = [turn_to(d, t, r_mqk, cs64, "swap64") for t in range(MOBA_T) for d in (mq, mk)]
                moba.insert(2, rows_step(norm, mv, r_mv, MOBA_H * 64, C0, QB))
                diff = [turn_to(d, t, r_dqk, cs32, "swap32") for t in range(DIFF_T) for d in (dq, dk)]
                diff.insert(2, rows_step(norm, dv, r_dv, DIFF_H * 64, C0, QB))
                stick_ = [plain_tile(norm, d[:, t, :], r_sqk, C0, N) for t in range(SB_T) for d in (sq_, sk)]
                stick_.insert(2, rows_step(norm, sv, r_sv, SB_H * 64, C0, QB))
                gates = [silu_tile(norm, gate[:, t, :], r_gate, C0, N) for t in range(8)]
                for _ in run(moba[:3], x):
                    pass
                units = []
                for t in range(MOBA_T):
                    units += [when(lambda t=t: len(r_mqk) >= 2 * t + 2, moba_unit(hd, qb))
                              for hd in (2 * t, 2 * t + 1) for qb in range(2)]
                for t in range(DIFF_T):
                    units += [when(lambda t=t: len(r_dqk) >= 2 * t + 2 and r_dv, diff_unit(hd, qb))
                              for hd in (2 * t, 2 * t + 1) for qb in range(2)]
                    units.append(when(lambda t=t: len(mixed_marks[d0 + t]) == 4, diff_norm(t)))
                for t in range(SB_T):
                    units += [when(lambda t=t: len(r_sqk) >= 2 * t + 2 and r_sv, stick_unit(hd)) for hd in (2 * t, 2 * t + 1)]
                merges = [when(lambda t=t: len(r_gate) > t and len(mixed_marks[t]) == [4, 5, 2][(t >= d0) + (t >= s0)],
                               merge(t)) for t in range(8)]
                weave(units, chain(run(moba[3:] + diff + stick_ + gates, x)), active=8)
                for u in merges:
                    for _ in u:
                        pass
                if l == 0:
                    mem_loaded = load_halves(mem_t, "mem_t", 0, SEQ, merged)
                norm = Norm(C0, N)
                add_to_h(other, KC, C0, N, norm=norm, feeds=(f"xattn{l}", x))

                r_q = []
                for _ in run([plain_tile(norm, mq[:, t, :] if t < 3 else mk[:, 0, :], r_q, C0, N) for t in range(X_H)], x):
                    pass
                cross_marks = [[] for _ in range(X_H)]

                def cross_unit(hd, qb):
                    q = (mq[:, hd, :] if hd < 3 else mk[:, 0, :])[:, qb * P:(qb + 1) * P]

                    def write(o, m):
                        w = copy_act(mix[:, hd, qb * P:(qb + 1) * P], o, [m])
                        cross_marks[hd].append(w)
                        if len(cross_marks[hd]) == 2:
                            split(mix[:, hd, :], cross_marks[hd], x, hd, C0, N, None)
                        return w
                    return attend(q, xk[l][:, hd, :], [r_q, r_xk[l]], P, SEQ, QB, None, None, 128 ** -0.5,
                                  [xv[l][:, j, hd * P:(hd + 1) * P] for j in range(2)], r_xv[l], (0, P), write)
                filler = iter(())
                if l == 0:
                    nm = feed_memory(1, other, mem_loaded)
                    filler = run(memory_tiles(1, nm, r_xk[1], r_xv[1]), other)
                weave([cross_unit(hd, qb) for hd in range(X_H) for qb in range(2)], filler, active=5)
                norm = Norm(C0, N)
                if l == 0:
                    add_to_h(x, 4, C0, N, norm=norm, feeds=("attn1", other), column=QB)
                else:
                    add_to_h(x, 4, C0, N, norm=norm)
                x, other = other, x

            norm.finish(D)
            for k in range(KC):
                h_ready[k] = fused(h[:, k, C0:TOK], h[:, k, C0:TOK], col("final", k), norm.rs[:, 0:N], ALU.mult, ALU.mult,
                                   [norm.mark, h_ready[k]])
            rstd.free[norm.r] = [h_ready[KC - 1]]

        norm = Norm(0, TOK)
        for k in range(KC):
            h_ready[k] = [h_ready[k], meta_loaded]
            feed(k, "f1g0", xa, 0, TOK, h_ready[k], urgent=(k == KC - 1))
            norm.square(h[:, k, :], h_ready[k])
        later.append(lambda n=norm: n.finish(D))

        def ffn(x, norm, c0, n, following, feeds, tag):
            with ExitStack() as s2:
                gated = Ring([sb(f"{tag}_gated{i}", [P, TOK], F32, s2) for i in range(3)])
                a = Split(sb(tag + "_hi", [P, FT, TOK], FR, s2), sb(tag + "_lo", [P, FT, TOK], FR, s2), FT)
                for j in range(FT):
                    b, o, mark = weight_tile(x, KC, c0, n)
                    flush()
                    g, gt, free = gated.take()
                    gm = norm.scale(gt[:, 0:n], o[:, 0:n], [mark, free])
                    acc.free[b] = [gm]
                    gm = activate(gt[:, 0:n], gt[:, 0:n], ACT.Silu, [gm])
                    b, o, mark = weight_tile(x, KC, c0, n)
                    s, y, free = whole.take()
                    ym = norm.scale(y[:, 0:n], o[:, 0:n], [mark, free])
                    acc.free[b] = [ym]
                    ym = pairwise(y[:, 0:n], y[:, 0:n], gt[:, 0:n], ALU.mult, [ym, gm])
                    gated.free[g] = [ym]
                    split(y[:, 0:n], ym, a, j, c0, n, s, urgent=(j == FT - 1))
                    settle()
                act.steps.append(([], lambda e: e.preload_act_table_set("natural_log_exp_and_others"), None, 0))
                add_to_h(a, FT, c0, n, 0.5, following, feeds, column=KB2 if tag == "ffn10" else None)

        def even_mixer(x, y_in, norm, following, feeds):
            with ExitStack() as s2:
                sb2 = lambda name, shape, dt=F32: sb("ev_" + name, shape, dt, s2)
                even = sb2("tables", [P, ins["even"].shape[1]])
                decay = Ring([sb2(f"decay{i}", [P, 432]) for i in range(3)])
                aq, ak, iq = (sb2(n, [P, 4, TOK]) for n in ("aq", "ak", "iq"))
                bq, bk = (Ring([sb2(f"{n}{i}", [P, TOK]) for i in range(2)]) for n in ("bq", "bk"))
                bv = Ring([sb2(f"bv{i}", [P, 3, P]) for i in range(3)])
                bg = Ring([sb2(f"bg{i}", [P, TOK]) for i in range(3)])
                ik, iw = sb2("ik", [P, TOK]), sb2("iw", [P, 3, IDX_H])
                av = sb2("av", [P, 3, 512])
                rest, bias = sb2("rest", [P, 3, TOK]), sb2("bias", [P, 3, TOK])
                best = Ring([sb2(f"best{i}", [P, 8]) for i in range(3)])
                scratch["raw"] = Ring([sb2(f"raw{i}", [P, TOK]) for i in range(3)])
                scratch["turn"] = Ring([sb2(f"turn{i}", [P, TOK]) for i in range(2)])
                ya = sb2("ya", [P, 4, TOK])
                yas = Split(sb2("ya_hi", [P, 4, TOK], FR), sb2("ya_lo", [P, 4, TOK], FR), 4)
                yb = Ring([sb2(f"yb{i}", [P, TOK]) for i in range(2)])
                tm = [sp.load(lambda e: e.dma_start(even[:, :], ins["even"]), tables, [h_ready[KC - 1]])]
                decay_sem = [Arrival(sem(f"s_decay{i}")) for i in range(3)]

                def table(name, c0=0, n=None):
                    at, width = ewhere[name]
                    return even[:, at + c0:at + (width if n is None else c0 + n)]

                r_i, r_iw, r_aq, r_ak, r_av = ([] for _ in range(5))
                for _ in run([plain_tile(norm, iq[:, t, :], r_i, 0, TOK) for t in range(4)]
                             + [plain_tile(norm, ik[:, :], r_i, 0, TOK)], x):
                    pass
                banks, mark = weight_rows(x, IDX_H, KB2)
                for (t0, tn), (b, o), j in zip(KB2, banks, range(3)):
                    m = scaled(iw[0:tn, j, :], o[0:tn, 0:IDX_H], norm.col[0:tn, j:j + 1], ALU.mult, [mark, norm.col_ready],
                               IDX_H ** -0.5 * 64 ** -0.5, ALU.mult)
                    acc.free[b] = [m]
                    r_iw.append(m)
                rstd_col.free[norm.col_slot] = [m]
                rq = (table("cosq"), table("sinq"), tm)
                rk = (table("cosk"), table("sink"), tm)
                a_tiles = [normed_tile(norm, aq[:, t, :], r_aq, "a_q", 0, TOK) for t in range(4)]
                a_tiles += [normed_tile(norm, ak[:, t, :], r_ak, "a_k", 0, TOK) for t in range(4)]
                a_tiles += [value_tile(norm, av, r_av, t * P) for t in range(4)]
                bias_ready = [None] * 3
                heads = {}
                width = [144, TOK, TOK]
                blocks = [[(0, P), (P, 16)], KB2, KB2]

                def index_unit(qb):
                    (q0, nq), nk = KB2[qb], width[qb]
                    adm = table("adm", qb * TOK, nk)[0:nq, :]
                    left = rest[0:nq, qb, 0:nk]
                    m = None
                    for hd in range(IDX_H):
                        t, p0 = hd // 2, (hd % 2) * 64
                        while not (score.open() and probs.open()):
                            yield True
                        b, o, free = score.take()
                        sm = product(o[0:nq, 0:nk], [(iq[p0:p0 + 64, t, q0:q0 + nq], ik[p0:p0 + 64, 0:nk])], [r_i, free])
                        pi, p, pfree = probs.take()
                        rm = activate(p[0:nq, 0:nk], o[0:nq, 0:nk], ACT.Relu, [sm, pfree])
                        score.free[b] = [rm]
                        m = fused(left, p[0:nq, 0:nk], iw[0:nq, qb, hd:hd + 1], left if hd else adm, ALU.mult, ALU.add,
                                  [rm, m, r_iw, tm])
                        probs.free[pi] = [m]
                        yield True
                    for n in range(TOP_K // 8):
                        bi, top, bfree = best.take()
                        m = dve.step(lambda e, top=top: e.max(top[0:nq, :], left), [m, bfree])
                        m = dve.step(lambda e, top=top: e.match_replace(left, top[0:nq, :], left, GONE), [m])
                        best.free[bi] = [m]
                        if n % 2:
                            yield True
                    m = scaled(bias[0:nq, qb, 0:nk], left, 0.5 * GONE, ALU.is_gt, [m], NEG, ALU.mult)
                    bias_ready[qb] = pairwise(bias[0:nq, qb, 0:nk], bias[0:nq, qb, 0:nk], adm, ALU.add, [m])

                ya_marks = [[] for _ in range(4)]

                def sparse_unit(hd, qb):
                    (q0, nq), nk = KB2[qb], width[qb]
                    t, p0 = hd // 2, (hd % 2) * 64

                    def write(o, m):
                        w = copy_act(ya[p0:p0 + 64, t, q0:q0 + nq], o, [m])
                        ya_marks[t].append(w)
                        if len(ya_marks[t]) == 6:
                            split(ya[:, t, :], ya_marks[t], yas, t, 0, TOK, None)
                        return w
                    return attend(aq[p0:p0 + 64, t, q0:q0 + nq], ak[p0:p0 + 64, t, 0:nk], [r_aq, r_ak], nq, nk, blocks[qb],
                                  bias[0:nq, qb, 0:nk], bias_ready[qb], 64 ** -0.5,
                                  [av[0:kn, j, hd * 64:(hd + 1) * 64] for j, (_, kn) in enumerate(blocks[qb])],
                                  r_av, (p0, 64), write)

                def retention_unit(hd):
                    p0 = (hd % 2) * 64
                    (qi, q), (ki, k), (vi, v), (gi, g), qk_marks, vg_marks, both = heads[hd]
                    marks, done = qk_marks + vg_marks, []
                    while not (decay.open() and score.open() and probs.open()):
                        yield True
                    di, dec, dfree = decay.take()
                    dm = sp.load(lambda e: e.dma_start(dec[:, :], ins["decay"][:, hd * 432:(hd + 1) * 432]), decay_sem[di],
                                 [dfree, tm])
                    b, o, free = score.take()

                    def scores(e):
                        at = 0
                        for k0, kn in KB2:
                            mm = e.matmul(o[0:kn, at:at + TOK - k0], k[p0:p0 + 64, k0:k0 + kn], q[p0:p0 + 64, k0:TOK],
                                          start=True, stop=True)
                            at += TOK - k0
                        return mm
                    sm = pe.step(scores, [marks, free])
                    done.append(sm)
                    pi, p, pfree = probs.take()
                    m1 = pairwise(p[:, 0:416], o[:, 0:416], dec[:, 0:416], ALU.mult, [sm, pfree, dm])
                    m2 = pairwise(p[0:16, 416:432], o[0:16, 416:432], dec[0:16, 416:432], ALU.mult, [sm, pfree, dm])
                    score.free[b], decay.free[di] = [m1, m2], [m1, m2]
                    yield True
                    while not yb.open():
                        yield True
                    b2, mx, free2 = mixed.take()

                    def values(e):
                        at = 0
                        for j, (k0, kn) in enumerate(KB2):
                            mm = e.matmul(mx[:, k0:TOK], v[0:kn, j, :], p[0:kn, at:at + TOK - k0],
                                          start=(j == 0), stop=(j == 2))
                            at += TOK - k0
                        return mm
                    vm = pe.step(values, [m1, m2, free2, marks])
                    probs.free[pi] = [vm]
                    done.append(vm)
                    yi, y, yfree = yb.take()
                    ym = copy_act(y[:, :], mx[:, 0:TOK], [vm, yfree])
                    mixed.free[b2] = [ym]
                    yield True
                    while not sumsq.open(2):
                        yield True
                    nm = Norm(0, TOK, 1, "ones")
                    nm.square(y[:, :], ym)
                    yield True
                    nm.finish(P)
                    s, z, zfree = whole.take()
                    m = pairwise(z[:, :], y[:, :], nm.rs[:, :], ALU.mult, [nm.mark, zfree])
                    nm.ring.free[nm.r], yb.free[yi] = [m], [m]
                    m = pairwise(z[:, :], z[:, :], g[:, :], ALU.mult, [m, marks])
                    split(z[:, :], m, y_in, hd, 0, TOK, s)
                    bv.free[vi], bg.free[gi] = [done[1]], [m]
                    both.append(done[0])
                    if len(both) == 2:
                        bq.free[qi] = bk.free[ki] = both

                def retention_tiles(t):
                    marks, both = [], []
                    while not (bq.open() and bk.open()):
                        yield True
                    (qi, q, qfree), (ki, k, kfree) = bq.take(), bk.take()
                    for tile in (turned_tile(norm, q[:, :], marks, rq, "swapr", 0, TOK, qfree),
                                 turned_tile(norm, k[:, :], marks, rk, "swapr", 0, TOK, kfree)):
                        for _ in run_on([tile], x):
                            yield True
                    for hd in (2 * t, 2 * t + 1):
                        vg = []
                        while not (bv.open() and bg.open()):
                            yield True
                        (vi, v, vfree), (gi, g, gfree) = bv.take(), bg.take()
                        for _ in run_on([value_tile(norm, v, vg, 0, vfree), silu_tile(norm, g[:, :], vg, 0, TOK, gfree)], x):
                            yield True
                        heads[hd] = (qi, q), (ki, k), (vi, v), (gi, g), marks, vg, both

                tiles = chain(*[retention_tiles(t) if kind == "b" else
                                run_on([a_tiles[j * 4 + t] for j in range(3)], x) for kind, t in EVEN_TILES])
                units = [index_unit(qb) for qb in range(3)]
                sparse = [when(lambda t=hd // 2, qb=qb: bias_ready[qb] and len(r_aq) > t and len(r_ak) > t
                               and len(r_av) > 2 * t + 1, lambda hd=hd, qb=qb: sparse_unit(hd, qb))
                          for hd in range(A_H) for qb in range(3)]
                retention = [when(lambda hd=hd: hd in heads and len(heads[hd][4]) == 2 and len(heads[hd][5]) == 3,
                                  lambda hd=hd: retention_unit(hd)) for hd in range(B_H)]
                for hd in range(B_H):
                    units += retention[hd:hd + 1] + sparse[3 * hd:3 * hd + 3]
                weave(units, tiles, active=EVEN_ACTIVE)
                add_to_h(Joined(yas, y_in), 12, 0, TOK, 1.0, following, feeds)

        def odd_mixer(x, norm, following, feeds):
            with ExitStack() as s2:
                sb2 = lambda name, shape, dt=F32: sb("od_" + name, shape, dt, s2)
                window, dmix = sb2("window", [P, 2, TOK]), sb2("mix", [P, 512])
                cq, ck, cv = sb2("cq", [P, 4, TOK]), sb2("ck", [P, TOK]), sb2("cv", [P, 3, P])
                scratch["raw"] = Ring([sb2(f"raw{i}", [P, TOK]) for i in range(2)])
                runs = Ring([sb2(f"run{i}", [P, 2, TOK]) for i in range(2)])
                pooled = Ring([sb2(f"pooled{i}", [P, SEQ]) for i in range(2)])
                yc = sb2("yc", [P, 4, SEQ])
                ycs = Split(sb2("yc_hi", [P, 4, TOK], FR), sb2("yc_lo", [P, 4, TOK], FR), 4)
                yds = Split(sb2("yd_hi", [P, 4, TOK], FR), sb2("yd_lo", [P, 4, TOK], FR), 4)
                tm = [sp.load(lambda e: e.dma_start(window[:, :, :], ins["window"].rearrange("p (b n) -> p b n", b=2)), tables,
                              [h_ready[KC - 1]]),
                      sp.load(lambda e: e.dma_start(dmix[:, :], ins["od_mix"]), tables)]
                tm = [tm[1]]
                r_ck, r_c, r_cv = [], [], []

                def pool_tile(g):
                    def gen(src):
                        b, o, mark = weight_tile(src, KC, 0, TOK)
                        flush()
                        r, rv, free = scratch["raw"].take()
                        m = norm.scale(rv[:, :], o[:, 0:TOK], [mark, free])
                        acc.free[b] = [m]
                        u, ru, ufree = runs.take()
                        have = rv[:, :]
                        for step in range(g + 1):
                            w, lo = 1 << step, (2 << step) - 1
                            to = ru[:, step % 2, :]
                            m = pairwise(to[:, lo:], have[:, lo:], have[:, lo - w:TOK - w], ALU.add, [m, ufree])
                            have = to
                        q, py, pfree = pooled.take()
                        m = fused(py[:, :], have[:, META:], 1.0 / (2 << g), rv[:, META:], ALU.mult, ALU.subtract, [m, pfree])
                        runs.free[u], scratch["raw"].free[r] = [m], [m]

                        def mix_groups():
                            b2, o2, free2 = acc.take()
                            mm = product(o2[:, 0:SEQ], [(dmix[:, g * P:(g + 1) * P], py[:, :])], [m, free2, tm])
                            pooled.free[q] = [mm]
                            s, y, sfree = whole.take()
                            ym = scaled(y[:, 0:SEQ], o2[:, 0:SEQ], col("d_scale", g), ALU.mult, [mm, sfree])
                            acc.free[b2] = [ym]
                            split(y[:, 0:SEQ], ym, yds, g, META, SEQ, s)
                        later.append(mix_groups)
                    return gen

                first = [normed_tile(norm, ck[:, :], r_ck, "c_k", 0, TOK), value_tile(norm, cv, r_cv, 0)]
                queries = [normed_tile(norm, cq[:, t, :], r_c, "c_q", 0, TOK) for t in range(4)]
                for _ in run(first + queries[:1], x):
                    pass
                yc_marks = [[] for _ in range(4)]

                def window_unit(j, half, qb):
                    p0, nk = half * 64, [144, TOK][qb]
                    blocks = [[(0, P), (P, 16)], KB2][qb]

                    def write(o, m):
                        w = copy_act(yc[p0:p0 + 64, j, qb * P:(qb + 1) * P], o, [m])
                        yc_marks[j].append(w)
                        if len(yc_marks[j]) == 4:
                            split(yc[:, j, :], yc_marks[j], ycs, j, META, SEQ, None)
                        return w
                    return attend(cq[p0:p0 + 64, j, META + qb * P:META + (qb + 1) * P], ck[p0:p0 + 64, 0:nk], [r_c, r_ck], P, nk,
                                  blocks, window[:, qb, 0:nk], tm, 64 ** -0.5,
                                  [cv[0:kn, i, p0:p0 + 64] for i, (_, kn) in enumerate(blocks)], r_cv, (p0, 64), write,
                                  sink=col("sinks", half * 4 + j))

                weave([when(lambda j=j: len(r_c) > j, window_unit(j, half, qb))
                       for j in range(4) for half in range(2) for qb in range(2)],
                      run(queries[1:] + [pool_tile(g) for g in range(4)], x))
                add_to_h(Joined(ycs, yds), KC, META, SEQ, 1.0, following, feeds)

        for_mix0, for_ffn20, for_ffn11, for_mix1, for_ffn21 = (Norm(*c) for c in 4 * [(0, TOK)] + [(META, SEQ)])
        ffn(xa, norm, 0, TOK, for_mix0, ("mixg0", xa), "ffn10")
        even_mixer(xa, xb, for_mix0, for_ffn20, ("f2g0", xa))
        ffn(xa, for_ffn20, 0, TOK, for_ffn11, ("f1g1", xa), "ffn20")
        ffn(xa, for_ffn11, 0, TOK, for_mix1, ("mixg1", xa), "ffn11")
        odd_mixer(xa, for_mix1, for_ffn21, ("f2g1", xa))
        ffn(xa, for_ffn21, META, SEQ, None, None, "ffn21")
        out_v = out.rearrange("p (c t) -> p c t", c=KC)
        for c in range(KC):
            sp.load(lambda e, c=c: e.dma_start(out_v[:, c, :], h[:, c, META:TOK]), out_sem, [h_ready[c]])
        sp.steps.append(([(out_sem.sem, out_sem.count)], None, None, 0))

        block = ctx.enter_context(nc.Block())

        block.sync(sp.play)
        block.scalar(act.play)
        block.vector(dve.play)
        block.gpsimd(pool.play)
        block.tensor(pe.play)


COLUMNS = {}


def column_layout():
    at = 0
    for name, width in ([(f"{n}{l}", KC) for n in ("attn", "xattn", "memg", "f1g", "mixg", "f2g") for l in range(DEPTH)]
                        + [("final", KC), ("head_gain", DEPTH), ("a_q", 1), ("a_k", 1), ("c_q", 1), ("c_k", 1),
                           ("sinks", C_H), ("d_scale", 4), ("lambda", DEPTH * 128)]):
        COLUMNS[name] = at
        at += width
    return at


N_COLUMNS = column_layout()


def pack_tiles(w):
    lead, (k, n) = w.shape[:-2], w.shape[-2:]
    a = w.reshape(*lead, k // P, P, n // P, P)
    j = len(lead)
    return np.ascontiguousarray(a.transpose(*range(j), j + 2, j + 1, j, j + 3)).reshape(*lead, n // P, P, k)


def pack_rows(w):
    lead, (k, n) = w.shape[:-2], w.shape[-2:]
    j = len(lead)
    a = w.reshape(*lead, k // P, P, n).transpose(*range(j), j + 1, j, j + 2)
    return np.ascontiguousarray(a).reshape(*lead, P, (k // P) * n)


def feature_major(a):
    return np.ascontiguousarray(a.T.reshape(-1, P, a.shape[0]).transpose(1, 0, 2)).reshape(P, -1)


def per_partition(v):
    return v.reshape(-1, P).T


def everywhere(v):
    return np.broadcast_to(v.reshape(1, -1), (P, v.size))


def layouts(a):
    w_in = a["w_in"]
    d = {}
    d["x_t"] = feature_major(a["x"][0])
    d["mem_t"] = feature_major(a["mem"][0])
    d["meta_t"] = feature_major(a["meta_tokens_2"])
    d["positions"] = np.ascontiguousarray(a["positions"])
    twice = lambda v: np.concatenate([v, v]).reshape(P, 1)
    columns = [per_partition(a[n][l]) for n in ("attn_norm_g", "xattn_norm_g", "mem_norm_g", "ffn1_norm_2",
                                                 "mix_norm_2", "ffn2_norm_2") for l in range(DEPTH)]
    columns += [per_partition(a["final_norm_g"])]
    columns += [twice(a["diff_head_norm_g"][l]) for l in range(DEPTH)]
    columns += [twice(a[n][0]) for n in ("ev_a_q_norm_2", "ev_a_k_norm_2", "od_c_q_norm_2", "od_c_k_norm_2")]
    columns += [everywhere(a["od_c_sinks_2"][0]), per_partition(a["od_d_scale_2"][0])]
    for l in range(DEPTH):
        columns += [everywhere(a[n][l]) for n in ("diff_lambda_q1", "diff_lambda_k1", "diff_lambda_q2", "diff_lambda_k2")]
    d["columns"] = np.ascontiguousarray(np.concatenate(columns, 1))
    assert d["columns"].shape[1] == N_COLUMNS
    d["w_in"] = pack_tiles(w_in)
    d["w_moba_v"] = pack_rows(w_in[:, :, 768:1152])
    d["w_diff_v"] = pack_rows(w_in[:, :, 2048:2304])
    d["w_sb_v"] = pack_rows(w_in[:, :, 3328:3712])
    d["w_out"] = pack_tiles(a["w_out"])
    d["w_xq"] = pack_tiles(a["w_xq"])
    d["w_xk"] = pack_tiles(a["w_xkv"][:, :, :512])
    d["w_xv"] = pack_rows(a["w_xkv"][:, :, 512:])
    d["w_xo"] = pack_tiles(a["w_xo"])
    for f in ("ffn1", "ffn2"):
        w = a[f + "_w_in_2"].reshape(DEPTH, D, 2, FT, P).transpose(0, 1, 3, 2, 4).reshape(DEPTH, D, 2 * D_FF)
        d[f + "_in"] = pack_tiles(w)
        d[f + "_out"] = pack_tiles(a[f + "_w_out_2"])
    ev = a["ev_w_in_2"][0]
    ik = ev[:, 2048:2112]
    d["ev_in"] = pack_tiles(np.concatenate([ev[:, 1536:2048], ik, ik, ev[:, 0:1536], ev[:, 2120:5192]], 1))
    d["ev_iw"] = pack_rows(ev[:, 2112:2120])
    d["ev_out"] = pack_tiles(a["ev_w_out_2"][0])
    od = a["od_w_in_2"][0]
    cq = od[:, 0:512].reshape(D, 2, 4, 64).transpose(0, 2, 1, 3).reshape(D, 512)
    d["od_in"] = pack_tiles(np.concatenate([cq, od[:, 512:1280]], 1))
    od_out = a["od_w_out_2"][0]
    co = od_out[0:512].reshape(2, 4, 64, D).transpose(1, 0, 2, 3).reshape(512, D)
    d["od_out"] = pack_tiles(np.concatenate([co, od_out[512:]], 0))
    d["od_mix"] = np.ascontiguousarray(a["od_d_mix_2"][0].transpose(1, 0, 2)).reshape(P, 512)
    d["consts"], where = stack_parts(constant_tables())
    d["even"], ewhere = stack_parts(even_tables())
    d["decay"] = decay_tables().astype(np.float32)
    d["window"] = window_tables().astype(np.float32)
    return d, where, ewhere


def kernel(**inputs):
    import concourse.bacc as _bacc
    from concourse import mybir as _mybir
    from concourse.bass_utils import run_bass_kernel_spmd as _run

    arrays, where, ewhere = layouts({k: np.asarray(v) for k, v in inputs.items()})
    nc = _bacc.Bacc("TRN2", target_bir_lowering=False, num_devices=1)
    feeds, ins = {}, {}
    for name, a in arrays.items():
        feeds[f"in_{name}"] = a
        ins[name] = nc.dram_tensor(f"in_{name}", a.shape, _mybir.dt.from_np(a.dtype), kind="ExternalInput").ap()
    out = nc.dram_tensor("out_t", (P, KC * SEQ), _mybir.dt.float32, kind="ExternalOutput").ap()
    program(nc, ins, out, where, ewhere)
    r = _run(nc, [feeds], core_ids=[0])
    got = r.results[0]["out_t"].reshape(P, KC, SEQ)
    return np.ascontiguousarray(got.transpose(2, 1, 0)).reshape(1, SEQ, D)
```
